# Optimizing a Trainium2 kernel written in Bass

```python
import math
import jax, jax.numpy as jnp
from jax import lax
import numpy as np

D_MODEL = 1024
BATCH = 1
SEQ = 2048
DEPTH = 1

D_MIX = D_MODEL
DN_WIDTH = D_MIX // 2
DN_HEADS = 4
DN_HEAD_DIM = DN_WIDTH // DN_HEADS
DN_CONV = 4
DN_CHUNK = 64
CF_WIDTH = D_MIX - DN_WIDTH
CF_KERNEL = 31
IN_COLS = 4 * DN_WIDTH + 2 * DN_HEADS + 2 * CF_WIDTH
N_GROUPS = 8
EXPERTS_PER_GROUP = 8
N_EXPERTS = N_GROUPS * EXPERTS_PER_GROUP
TOP_K = 2
D_EXPERT = D_MODEL // 2
MOE_BLOCK = 128
EPS = 1e-6
N_MOD = 6

kernel_name = "hybrid_deltanet_conformer_hmoe_block"

F32 = jnp.float32

def rms_norm(x, w):
    xf = x.astype(F32)
    y = xf * lax.rsqrt(jnp.mean(xf * xf, axis=-1, keepdims=True) + EPS)
    return (y * w.astype(F32)).astype(x.dtype)

def layer_norm(x, w, b):
    xf = x.astype(F32)
    mu = jnp.mean(xf, axis=-1, keepdims=True)
    xc = xf - mu
    var = jnp.mean(xc * xc, axis=-1, keepdims=True)
    return (xc * lax.rsqrt(var + EPS) * w.astype(F32) + b.astype(F32)).astype(x.dtype)

def l2norm(x):
    return x * lax.rsqrt(jnp.sum(x * x, axis=-1, keepdims=True) + EPS)

def causal_depthwise_conv(x, w):
    K, C = w.shape
    return lax.conv_general_dilated(
        x, w[:, None, :].astype(x.dtype), window_strides=(1,), padding=[(K - 1, 0)],
        dimension_numbers=("NWC", "WIO", "NWC"), feature_group_count=C)

def gated_delta_rule(q, k, v, g, beta):
    B, S, H, dk = q.shape
    dv = v.shape[-1]
    C = DN_CHUNK
    N = S // C

    def chunks(t):
        t = jnp.moveaxis(t, 2, 1)
        return t.reshape((B, H, N, C) + t.shape[3:])

    q, k, v, g, beta = chunks(q), chunks(k), chunks(v), chunks(g), chunks(beta)
    q = q * (dk ** -0.5)
    g = jnp.cumsum(g, axis=-1)
    causal = jnp.tril(jnp.ones((C, C), dtype=bool))
    strict = jnp.tril(jnp.ones((C, C), dtype=bool), -1)
    decay = jnp.exp(jnp.where(causal, g[..., :, None] - g[..., None, :], -jnp.inf))
    k_beta = k * beta[..., None]
    a = jnp.where(strict, jnp.einsum("bhncd,bhnsd->bhncs", k_beta, k) * decay, 0.0)
    rhs = jnp.concatenate([v * beta[..., None], k_beta * jnp.exp(g)[..., None]], axis=-1)
    sol = lax.linalg.triangular_solve(a, rhs, left_side=True, lower=True, unit_diagonal=True)
    u, w = sol[..., :dv], sol[..., dv:]
    attn = jnp.einsum("bhncd,bhnsd->bhncs", q, k) * decay
    q_g = q * jnp.exp(g)[..., None]
    g_last = g[..., -1]
    k_dec = k * jnp.exp(g_last[..., None] - g)[..., None]

    def step(state, inp):
        u_c, w_c, attn_c, qg_c, kd_c, gl_c = inp
        v_new = u_c - jnp.einsum("bhcd,bhde->bhce", w_c, state)
        o = jnp.einsum("bhcd,bhde->bhce", qg_c, state) + jnp.einsum("bhcs,bhse->bhce", attn_c, v_new)
        state = state * jnp.exp(gl_c)[..., None, None] + jnp.einsum("bhcd,bhce->bhde", kd_c, v_new)
        return state, o

    xs = tuple(jnp.moveaxis(t, 2, 0) for t in (u, w, attn, q_g, k_dec, g_last))
    state0 = jnp.zeros((B, H, dk, dv), F32)
    _, o = lax.scan(step, state0, xs)
    o = jnp.moveaxis(o, 0, 2).reshape(B, H, S, dv)
    return jnp.moveaxis(o, 1, 2)

def hybrid_mixer(h, w_in, dn_conv_w, dn_a_log, dn_dt_bias, dn_norm_w,
                 cf_pw1_b, cf_dw_w, cf_dw_b, cf_ln_w, cf_ln_b, w_out):
    B, S, _ = h.shape
    proj = jnp.einsum("bsd,de->bse", h, w_in)
    qkv, z, b_logit, a_logit, cf_in = jnp.split(
        proj, [3 * DN_WIDTH, 4 * DN_WIDTH, 4 * DN_WIDTH + DN_HEADS, 4 * DN_WIDTH + 2 * DN_HEADS], axis=-1)

    qkv = jax.nn.silu(causal_depthwise_conv(qkv, dn_conv_w))
    q, k, v = jnp.split(qkv.astype(F32), 3, axis=-1)
    q = l2norm(q.reshape(B, S, DN_HEADS, DN_HEAD_DIM))
    k = l2norm(k.reshape(B, S, DN_HEADS, DN_HEAD_DIM))
    v = v.reshape(B, S, DN_HEADS, DN_HEAD_DIM)
    beta = jax.nn.sigmoid(b_logit.astype(F32))
    g = -jnp.exp(dn_a_log.astype(F32)) * jax.nn.softplus(a_logit.astype(F32) + dn_dt_bias.astype(F32))
    o = gated_delta_rule(q, k, v, g, beta)
    zg = jax.nn.silu(z.astype(F32).reshape(B, S, DN_HEADS, DN_HEAD_DIM))
    o = (rms_norm(o, dn_norm_w) * zg).reshape(B, S, DN_WIDTH).astype(h.dtype)

    cf = jax.nn.glu(cf_in + cf_pw1_b, axis=-1)
    cf = causal_depthwise_conv(cf, cf_dw_w) + cf_dw_b
    cf = jax.nn.silu(layer_norm(cf, cf_ln_w, cf_ln_b))

    mixed = jnp.concatenate([o, cf.astype(h.dtype)], axis=-1)
    return jnp.einsum("bsd,de->bse", mixed, w_out)

def hierarchical_moe(h, w_router_group, b_router_group, w_router_expert, b_router_expert,
                     w_gate, w_up, w_down):
    B, S, D = h.shape
    T = B * S
    xt = h.reshape(T, D)
    grp_prob = jax.nn.softmax(jnp.dot(xt, w_router_group).astype(F32) + b_router_group.astype(F32), axis=-1)
    grp_p, grp_idx = lax.top_k(grp_prob, 1)
    exp_logits = (jnp.dot(xt, w_router_expert).astype(F32) + b_router_expert.astype(F32))
    exp_logits = exp_logits.reshape(T, N_GROUPS, EXPERTS_PER_GROUP)
    sel = jnp.take_along_axis(exp_logits, grp_idx[:, :, None], axis=1)[:, 0]
    top_p, top_local = lax.top_k(jax.nn.softmax(sel, axis=-1), TOP_K)
    top_p = top_p / jnp.sum(top_p, axis=-1, keepdims=True)
    weights = grp_p * top_p
    expert_id = grp_idx * EXPERTS_PER_GROUP + top_local

    n_assign = T * TOP_K
    flat_e = expert_id.reshape(-1)
    flat_w = weights.reshape(-1)
    flat_tok = jnp.arange(n_assign, dtype=jnp.int32) // TOP_K
    order = jnp.argsort(flat_e)
    sorted_e = flat_e[order]
    counts = jnp.bincount(flat_e, length=N_EXPERTS)
    padded = (counts + MOE_BLOCK - 1) // MOE_BLOCK * MOE_BLOCK
    start = jnp.cumsum(counts) - counts
    pend = jnp.cumsum(padded)
    pstart = pend - padded
    dest = pstart[sorted_e] + jnp.arange(n_assign, dtype=jnp.int32) - start[sorted_e]
    n_blocks = -(-n_assign // MOE_BLOCK) + N_EXPERTS
    rows = n_blocks * MOE_BLOCK
    row_tok = jnp.zeros((rows,), jnp.int32).at[dest].set(flat_tok[order])
    row_w = jnp.zeros((rows,), F32).at[dest].set(flat_w[order])
    block_start = jnp.arange(n_blocks, dtype=jnp.int32) * MOE_BLOCK
    block_e = jnp.minimum(jnp.sum(pend[None, :] <= block_start[:, None], axis=1), N_EXPERTS - 1)

    def run_block(args):
        tok, e = args
        xb = xt[tok]
        hid = jax.nn.silu(jnp.dot(xb, w_gate[e])) * jnp.dot(xb, w_up[e])
        return jnp.dot(hid, w_down[e])

    y = lax.map(run_block, (row_tok.reshape(n_blocks, MOE_BLOCK), block_e))
    y = y.reshape(rows, D) * row_w[:, None].astype(y.dtype)
    out = jnp.zeros((T, D), y.dtype).at[row_tok].add(y)
    return out.reshape(B, S, D)

def setup_inputs(seed: int = 0) -> dict:
    key = jax.random.key(seed)
    ks = jax.random.split(key, 32)
    L, D = DEPTH, D_MODEL
    nrm = lambda k, shape, s: jax.random.normal(k, shape, F32) * s
    gain = lambda k, shape: 1.0 + 0.02 * jax.random.normal(k, shape, F32)
    dt = jnp.exp(jax.random.uniform(ks[7], (L, DN_HEADS), F32) * (math.log(0.1) - math.log(1e-3)) + math.log(1e-3))
    return {
        "x": nrm(ks[0], (BATCH, SEQ, D), 1.0),
        "c": nrm(ks[1], (BATCH, D), 1.0),
        "w_ada": nrm(ks[2], (L, D, N_MOD * D), 0.5 * D ** -0.5),
        "b_ada": nrm(ks[3], (L, N_MOD * D), 0.02),
        "norm_pre_mix": gain(ks[4], (L, D)),
        "norm_post_mix": gain(ks[5], (L, D)),
        "w_in": nrm(ks[6], (L, D, IN_COLS), D ** -0.5),
        "dn_conv_w": nrm(ks[8], (L, DN_CONV, 3 * DN_WIDTH), DN_CONV ** -0.5),
        "dn_a_log": jnp.log(jax.random.uniform(ks[9], (L, DN_HEADS), F32, 1.0, 16.0)),
        "dn_dt_bias": dt + jnp.log(-jnp.expm1(-dt)),
        "dn_norm_w": gain(ks[10], (L, DN_HEAD_DIM)),
        "cf_pw1_b": nrm(ks[11], (L, 2 * CF_WIDTH), 0.02),
        "cf_dw_w": nrm(ks[12], (L, CF_KERNEL, CF_WIDTH), CF_KERNEL ** -0.5),
        "cf_dw_b": nrm(ks[13], (L, CF_WIDTH), 0.02),
        "cf_ln_w": gain(ks[14], (L, CF_WIDTH)),
        "cf_ln_b": nrm(ks[15], (L, CF_WIDTH), 0.02),
        "w_out": nrm(ks[16], (L, D_MIX, D), D_MIX ** -0.5),
        "norm_pre_ffn": gain(ks[17], (L, D)),
        "norm_post_ffn": gain(ks[18], (L, D)),
        "w_router_group": nrm(ks[19], (L, D, N_GROUPS), D ** -0.5),
        "b_router_group": nrm(ks[20], (L, N_GROUPS), 0.01),
        "w_router_expert": nrm(ks[21], (L, D, N_EXPERTS), D ** -0.5),
        "b_router_expert": nrm(ks[22], (L, N_EXPERTS), 0.01),
        "w_gate": nrm(ks[23], (L, N_EXPERTS, D, D_EXPERT), D ** -0.5),
        "w_up": nrm(ks[24], (L, N_EXPERTS, D, D_EXPERT), D ** -0.5),
        "w_down": nrm(ks[25], (L, N_EXPERTS, D_EXPERT, D), D_EXPERT ** -0.5),
    }

def reference(x, c, w_ada, b_ada, norm_pre_mix, norm_post_mix, w_in, dn_conv_w, dn_a_log, dn_dt_bias,
              dn_norm_w, cf_pw1_b, cf_dw_w, cf_dw_b, cf_ln_w, cf_ln_b, w_out, norm_pre_ffn, norm_post_ffn,
              w_router_group, b_router_group, w_router_expert, b_router_expert, w_gate, w_up, w_down):
    c_act = jax.nn.silu(c)
    for l in range(DEPTH):
        mod = jnp.einsum("bd,de->be", c_act, w_ada[l]) + b_ada[l]
        shift1, scale1, gate1, shift2, scale2, gate2 = jnp.split(mod[:, None, :], N_MOD, axis=-1)
        h = rms_norm(x, norm_pre_mix[l]) * (1.0 + scale1) + shift1
        h = hybrid_mixer(h, w_in[l], dn_conv_w[l], dn_a_log[l], dn_dt_bias[l], dn_norm_w[l],
                         cf_pw1_b[l], cf_dw_w[l], cf_dw_b[l], cf_ln_w[l], cf_ln_b[l], w_out[l])
        x = x + gate1 * rms_norm(h, norm_post_mix[l])
        h = rms_norm(x, norm_pre_ffn[l]) * (1.0 + scale2) + shift2
        h = hierarchical_moe(h, w_router_group[l], b_router_group[l], w_router_expert[l], b_router_expert[l],
                             w_gate[l], w_up[l], w_down[l])
        x = x + gate2 * rms_norm(h, norm_post_ffn[l])
    return x


_drawn_inputs = setup_inputs


def setup_inputs(seed=0):
    import zlib

    import numpy as np

    out = dict(_drawn_inputs(seed))
    spreads = {}
    factors = {'cf_ln_b': 2.693, 'norm_post_ffn': 8.0, 'b_router_expert': 2.887}
    for name, (base, spread) in spreads.items():
        noise = np.random.default_rng([zlib.crc32(name.encode()), seed]).standard_normal(out[name].shape)
        drawn = base * np.exp(spread * noise) if base else spread * noise
        out[name] = __import__('jax').numpy.asarray(drawn.astype(out[name].dtype))
    for name, factor in factors.items():
        out[name] = (out[name] * factor).astype(out[name].dtype)
    return out
```

```python
from contextlib import ExitStack

import numpy as np
import concourse.bass as bass
from concourse import mybir
from concourse.alu_op_type import AluOpType as ALU

P = 128
SEQ, D = 2048, 1024
NCH = SEQ // P
KD = D // P
HEADS, HD = 4, 128
DNW = HEADS * HD
CFW = D - DNW
CFG = CFW // P
DNT, CFT = 4, 31
QKVG = 3 * DNW // P
COL_Z, COL_BA, COL_CFA, COL_CFB = 3 * DNW, 4 * DNW, 4 * DNW + 2 * HEADS, 4 * DNW + 2 * HEADS + CFW
IN_COLS = COL_CFB + CFW
LEVELS = 7
NG, EPG = 8, 8
NE = NG * EPG
NR = NG + NE
DE = 512
KE = DE // P
EPS = 1e-6
ROOT_D = float(D) ** 0.5
BLOCKS = 2 * SEQ // P + NE
ROWS = BLOCKS * P
FREE_ROW = 1 << 14
SLOTS = 3
GU_COLS, DN_COLS = KD * 2 * DE, KE * D

SCRATCH = "Internal"

F32, BF16, I32, U32 = mybir.dt.float32, mybir.dt.bfloat16, mybir.dt.int32, mybir.dt.uint32
ACT = mybir.ActivationFunctionType
AXX = mybir.AxisListType.X

CH_C, CH_NPRE, CH_NFFN = 0, KD, 2 * KD
CH_DNW = 3 * KD
CH_CFB = CH_DNW + QKVG * DNT
CH_CFW = CH_CFB + 2 * CFG
CH_DWB = CH_CFW + CFG * CFT
CH_LNW, CH_LNB = CH_DWB + CFG, CH_DWB + 2 * CFG
CH_COLS = CH_DWB + 3 * CFG
C_ID, C_UI, C_US, C_LS, C_ONE, C_LV = 0, 1, 2, 3, 4, 5
C_MATS = 5 + LEVELS
R_ADA, R_NPM, R_NPF = 0, 6 * D, 7 * D
R_DNN = 8 * D
R_ALOG, R_DT, R_RB = R_DNN + HD, R_DNN + HD + HEADS, R_DNN + HD + 2 * HEADS
R_COLS = R_RB + NR


def over_cols(ap, n):
    return ap.unsqueeze(2).to_broadcast([ap.shape[0], ap.shape[1], n])


def over_heads(ap, n):
    return ap.unsqueeze(1).to_broadcast([ap.shape[0], n, ap.shape[1]])


def build_setup(nc, ctx, t, dram):
    with ExitStack() as own:
        def sb(name, shape, dt=F32):
            return own.enter_context(nc.sbuf_tensor(name, shape, dt))

        def sem(name):
            return t.ctx.enter_context(nc.semaphore(name))

        mod = sb("mod", [P, 6 * D])
        wa = [sb(f"wa{s}", [P, KD, 512]) for s in range(2)]
        cact = sb("cact", [P, KD])
        cbc = sb("cbc", [P, KD, P])
        g2 = sb("g2", [P, D])
        cols = sb("modcols", [P, 4, KD])
        pa = [own.enter_context(nc.psum_tensor(f"ada_ps{s}", [P, 512], F32)) for s in range(2)]
        pt = [own.enter_context(nc.psum_tensor(f"modT_ps{s}", [P, KD, P], F32)) for s in range(2)]
        params_in, rows_in, w_in_loaded = sem("params_in"), sem("rows_in"), sem("w_in_loaded")
        wa_in = [sem("wa_in0"), sem("wa_in1")]
        c_silu, c_spread, ada_ps, ada_added = sem("c_silu"), sem("c_spread"), sem("ada_ps"), sem("ada_added")
        modT_ps, modT_read, tail, decay_exp = sem("modT_ps"), sem("modT_read"), sem("setup_tail"), sem("decay_exp")
        g2_out = sem("g2_out")
        NA = 6 * D // 512
        COLS = (0, 1, 3, 4)

        block = own.enter_context(nc.Block())

        @block.sync
        def _(sp):
            sp.dma_start(t.chp[:], dram["chp"]).then_inc(params_in, 16)
            sp.dma_start(t.cst[:], dram["cst"]).then_inc(params_in, 16)
            for n in range(NA):
                if n >= 2:
                    sp.wait_ge(ada_ps, n - 1)
                sp.dma_start(wa[n % 2][:], dram["w_ada"].rearrange("(k p) n -> p k n", p=P)[
                    :, :, n * 512:(n + 1) * 512]).then_inc(wa_in[n % 2], 16)
            sp.wait_ge(tail, 2)
            sp.dma_start(dram["g2"], g2[0:1, :]).then_inc(g2_out, 16)
            sp.wait_ge(g2_out, 16)

        @block.scalar
        def _(act):
            def row(a, n):
                return dram["rows"][:, a:a + n].to_broadcast([P, n])

            act.dma_start(mod[:], row(R_ADA, 6 * D)).then_inc(rows_in, 16)
            act.dma_start(t.G1[:], row(R_NPM, D)).then_inc(rows_in, 16)
            act.dma_start(g2[:], row(R_NPF, D)).then_inc(rows_in, 16)
            act.dma_start(t.dnn[:], row(R_DNN, HD)).then_inc(rows_in, 16)
            act.dma_start(t.gaterow[:], row(R_ALOG, 2 * HEADS)).then_inc(rows_in, 16)
            act.dma_start(t.rbias[:], row(R_RB, NR)).then_inc(rows_in, 16)
            act.wait_ge(params_in, 32)
            act.activation(cact[:], t.chp[:, CH_C:CH_C + KD], ACT.Silu).then_inc(c_silu, 1)
            for k in range(KD):
                act.dma_start(t.win[:, k, :], dram["w_in"][:, k, :]).then_inc(w_in_loaded, 16)
            act.dma_start(t.wout[:], dram["w_out"]).then_inc(w_in_loaded, 16)
            act.dma_start(t.wr[:], dram["w_r"]).then_inc(w_in_loaded, 16)
            act.wait_ge(rows_in, 96)
            act.activation(t.gaterow[:, 0:HEADS], t.gaterow[:, 0:HEADS], ACT.Exp).then_inc(decay_exp, 1)
            act.wait_ge(w_in_loaded, 16 * (KD + 2))

        @block.tensor
        def _(pe):
            pe.wait_ge(c_spread, 1)
            for n in range(NA):
                pe.wait_ge(wa_in[n % 2], 16 * (n // 2 + 1))
                if n >= 2:
                    pe.wait_ge(ada_added, n - 1)
                for k in range(KD):
                    mm = pe.matmul(pa[n % 2][:], cbc[:, k, :], wa[n % 2][:, k, :], start=(k == 0), stop=(k == KD - 1))
                mm.then_inc(ada_ps, 1)
            pe.wait_ge(ada_added, NA)
            for q, m in enumerate(COLS):
                if q >= 2:
                    pe.wait_ge(modT_read, q - 1)
                for k in range(KD):
                    part = mod[:, m * D:(m + 1) * D]
                    part = part[:, k * P:(k + 1) * P] if m < 3 else part.rearrange("p (q k) -> p k q", k=KD)[:, k, :]
                    mm = pe.transpose(pt[q % 2][:, k, :], part, t.cst[:, C_ID, :])
                mm.then_inc(modT_ps, 1)

        @block.vector
        def _(dve):
            dve.wait_ge(c_silu, 1)
            dve.tensor_copy(cbc[:], over_cols(cact[:], P)).then_inc(c_spread, 1)
            dve.wait_ge(rows_in, 96)
            for n in range(NA):
                dve.wait_ge(ada_ps, n + 1)
                m = mod[:, n * 512:(n + 1) * 512]
                dve.tensor_tensor(m, pa[n % 2][:], m, ALU.add).then_inc(ada_added, 1)
            dve.wait_ge(ada_added, NA)
            dve.scalar_tensor_tensor(t.G1[:], t.G1[:], ROOT_D, mod[:, 2 * D:3 * D], ALU.mult, ALU.mult).then_inc(tail, 1)
            dve.scalar_tensor_tensor(g2[:], g2[:], ROOT_D, mod[:, 5 * D:6 * D], ALU.mult, ALU.mult).then_inc(tail, 1)
            for q in range(4):
                dve.wait_ge(modT_ps, q + 1)
                dve.tensor_copy(cols[:, q, :], pt[q % 2][:, :, 0]).then_inc(modT_read, 1)
            dve.wait_ge(modT_read, 4)
            dve.scalar_tensor_tensor(t.A1[:], cols[:, 1, :], 1.0, t.chp[:, CH_NPRE:CH_NPRE + KD], ALU.add, ALU.mult)
            dve.scalar_tensor_tensor(t.A2[:], cols[:, 3, :], 1.0, t.chp[:, CH_NFFN:CH_NFFN + KD], ALU.add, ALU.mult)
            dve.tensor_copy(t.B1[:], cols[:, 0, :])
            dve.tensor_copy(t.B2[:], cols[:, 2, :])
            dve.tensor_scalar(t.halfb[:], t.chp[:, CH_CFB:CH_CFB + 2 * CFG], 0.5, None, ALU.mult)
            dve.wait_ge(decay_exp, 1)
            dve.tensor_scalar(t.nega[:], t.gaterow[:, 0:HEADS], -1.0, None, ALU.mult)
            dve.tensor_scalar(t.dnn[:], t.dnn[:], float(HD) ** 0.5, None, ALU.mult)
            dve.memset(t.babias[:, 0:HEADS], 0.0)
            dve.tensor_copy(t.babias[:, HEADS:2 * HEADS], t.gaterow[:, HEADS:2 * HEADS]).then_inc(tail, 1)
            dve.wait_ge(tail, 3)


def build_mixer(nc, t, dram):
    sems = []
    with ExitStack() as own:
        def sb(name, shape, dt=F32):
            return own.enter_context(nc.sbuf_tensor(name, shape, dt))

        def sem(name):
            sems.append(nc.alloc_semaphore(name))
            return sems[-1]

        xin = sb("xin", [P, D])
        junk = sb("junk", [P, D], BF16)
        hT = sb("hT", [P, KD, P])
        pre = sb("pre", [P, QKVG, DNT - 1 + P])
        cfpre = sb("cfpre", [P, CFG, CFT - 1 + P])
        cv = sb("cv", [P, QKVG, P])
        cvf = sb("cvf", [P, CFG, P])
        glut = sb("glut", [P, CFG, P])
        zg = sb("zg", [P, HEADS, HD])
        small = sb("small", [P, 96])
        qkvT = sb("qkvT", [P, QKVG, P])
        h2n = sb("h2n", [P, D])
        sq = h2n[:].rearrange("p (g c) -> p g c", g=2 * HEADS)
        x1 = sb("x1", [P, D])
        mixT = sb("mixT", [P, KD, P])
        khat, khatT = sb("khat", [P, HEADS, HD]), sb("khatT", [P, HEADS, P])
        kw, bv = sb("kw", [P, HEADS, HD]), sb("bv", [P, HEADS, HD])
        EU, KT, attnT = sb("EU", [P, HEADS, P]), sb("KT", [P, HEADS, P]), sb("attnT", [P, HEADS, P])
        Kl = [sb("Kl0", [P, HEADS, P]), sb("Kl1", [P, HEADS, P])]
        T, N, Pm, S = (sb(n, [P, HEADS, P]) for n in ("T", "N", "Pm", "S"))
        xc = sb("xc", [P, CFG, P])
        gU, nwT, vn, o1, o2 = Kl[1], Kl[0], Pm, KT, T
        lnsq = sq[:, 0:CFG, :]
        lnr = sb("lnr", [P, P])
        (ss0, rs0, ss1, rs1, ss2, rs2, v0, v1, v2) = (small[:, n:n + 1] for n in range(9))
        ssn, rqk = small[:, 10:18], small[:, 18:26]
        bal, en, e8 = small[:, 26:34], small[:, 34:42], small[:, 42:50]
        l4, sp4, g4 = small[:, 50:54], small[:, 54:58], small[:, 58:62]
        beta, nbe = small[:, 62:66], small[:, 66:70]
        ex = small[:, 70:82]
        oss, orr = small[:, 82:86], small[:, 86:90]
        eps_d, eps_hd2 = small[:, 90:91], small[:, 91:95]
        hp = sb("half_pow", [P, P])
        scr = sb("scr", [P, 16])
        lgs = sb("lgs", [P, NR])

        def ps(name, shape):
            return own.enter_context(nc.psum_tensor(name, shape, F32))

        wide = ps("wide_ps", [P, D])
        pj = [ps("pj0_ps", [P, 4, P]), ps("pj1_ps", [P, 4, P])]
        misc = ps("misc_ps", [P, 512])
        b5, b6, b7 = (ps(f"dn{n}_ps", [P, HEADS, P]) for n in range(3))
        wideT = wide[:].rearrange("p (k c) -> p k c", k=KD)
        m_ssq, m_gate, m_ba = misc[:, 0:8], misc[:, 8:20], misc[:, 24:32]
        m_mean, m_var, m_lg = misc[:, 128:256], misc[:, 256:384], misc[:, 384:384 + NR]

        (x_loaded, x_ss, x_var, x_rstd, xn_ready, xnT_ps, hT_ready) = map(sem, (
            "x_loaded", "x_ss", "x_var", "x_rstd", "xn_ready", "xnT_ps", "hT_ready"))
        (cfa_ps, cfb_ps, q_ps, k_ps, v_ps, z_ps, ba_ps) = map(sem, (
            "cfa_ps", "cfb_ps", "q_ps", "k_ps", "v_ps", "z_ps", "ba_ps"))
        (cfa_evac, cfb_evac, q_evac, k_evac, v_evac, z_evac) = map(sem, (
            "cfa_evac", "cfb_evac", "q_evac", "k_evac", "v_evac", "z_evac"))
        halo_dn, halo_cf, glu_done, cf_tap, dn_tap, z_ready = map(sem, (
            "halo_dn", "halo_cf", "glu_done", "cf_tap", "dn_tap", "z_ready"))
        (ba_biased, ba_neg, ba_exp, ba_ln, beta_den, softplus, g_ready, gU_ready, dec_ps, gates_ps,
         dec_exp, gates_exp, EU_ready, nbe_ready) = map(sem, (
            "ba_biased", "ba_neg", "ba_exp", "ba_ln", "beta_den", "softplus", "g_ready", "gU_ready",
            "dec_ps", "gates_ps", "dec_exp", "gates_exp", "EU_ready", "nbe_ready"))
        (qkv_act, qk_sq, kv_ps, ssq_ps, ssn_ready, rqk_ready, khat_ready, bv_ready, kw_ready, kdec_ready,
         khatT_ps, khatT_ready, kk_ps, attn_ps, KT_ready, attnT_ready) = map(sem, (
            "qkv_act", "qk_sq", "kv_ps", "ssq_ps", "ssn_ready", "rqk_ready", "khat_ready", "bv_ready",
            "kw_ready", "kdec_ready", "khatT_ps", "khatT_ready", "kk_ps", "attn_ps", "KT_ready",
            "attnT_ready"))
        mask_done, p1_ps, p_ready, tp_ps, t_ready, pn_ps, n_ready = map(sem, (
            "mask_done", "p1_ps", "p_ready", "tp_ps", "t_ready", "pn_ps", "n_ready"))
        (wT_ps, nwT_ready, oS_ps, vn_ps, vn_ready, oa_ps, dS_ps, S_decayed, S_ready, o_step, o_ss, o_rs,
         o_gated, oT_ps, oT_ready) = map(sem, (
            "wT_ps", "nwT_ready", "oS_ps", "vn_ps", "vn_ready", "oa_ps", "dS_ps", "S_decayed", "S_ready",
            "o_step", "o_ss", "o_rs", "o_gated", "oT_ps", "oT_ready"))
        (mean_ps, xc_ready, xc_sq, var_ps, lnr_var, lnr_ready, cfn_ready, cf_ready) = map(sem, (
            "mean_ps", "xc_ready", "xc_sq", "var_ps", "lnr_var", "lnr_ready", "cfn_ready", "cf_ready"))
        (xr_loaded, mix_ps, mix_ss, mix_var, mix_rstd, mix_normed, x1_ready, x1_ss, x1_var, x1_rstd,
         h2n_ready, x1_out, h2n_out, h2T_ps, h2T_ready, lg_ps, lg_ready, lg_out, pstep, consts_set) = map(sem, (
            "xr_loaded", "mix_ps", "mix_ss", "mix_var", "mix_rstd", "mix_normed", "x1_ready", "x1_ss",
            "x1_var", "x1_rstd", "h2n_ready", "x1_out", "h2n_out", "h2T_ps", "h2T_ready", "lg_ps",
            "lg_ready", "lg_out", "pool_step", "consts_set"))

        ident = t.cst[:, C_ID, :]
        xd = dram["x"].rearrange("(n p) d -> n p d", p=P)
        x1d = dram["x1"].rearrange("(n p) d -> n p d", p=P)
        h2d = dram["h2"].rearrange("(n p) d -> n p d", p=P)

        def chunk(ap, i):
            return ap[bass.ds(i, 1)].rearrange("o p d -> (o p) d")

        ITEMS = ((COL_CFA, 1, cfa_ps, v_evac, 0), (COL_CFB, 0, cfb_ps, z_evac, 0),
                 (0, 1, q_ps, cfa_evac, 1), (DNW, 0, k_ps, cfb_evac, 1), (2 * DNW, 1, v_ps, q_evac, 1))

        block = own.enter_context(nc.Block())

        @block.sync
        def _(sp):
            def load_x(j):
                sp.wait_ge(xnT_ps, j)
                sp.dma_start(xin[:], chunk(xd, j)).then_inc(x_loaded, 16)

            def load_xr(i):
                sp.wait_ge(x1_out, 16 * i)
                sp.wait_ge(x1_rstd, i)
                sp.wait_ge(h2n_ready, i)
                sp.dma_start(x1[:], chunk(xd, i)).then_inc(xr_loaded, 16)

            def stores(i):
                sp.wait_ge(x1_ready, i + 1)
                sp.dma_start(chunk(x1d, i), x1[:]).then_inc(x1_out, 16)
                sp.wait_ge(h2n_ready, i + 1)
                sp.dma_start(chunk(h2d, i), h2n[:]).then_inc(h2n_out, 16)
                sp.wait_ge(lg_ready, i + 1)
                sp.dma_start(chunk(dram["lg"], i), lgs[:]).then_inc(lg_out, 16)

            load_x(0)
            load_x(1)
            with sp.Fori(0, NCH - 2) as i:
                load_xr(i)
                load_x(i + 2)
                stores(i)
            for i in (NCH - 2, NCH - 1):
                load_xr(i)
                stores(i)
            sp.wait_ge(x1_out, 16 * NCH)
            sp.wait_ge(h2n_out, 16 * NCH)
            sp.wait_ge(lg_out, 16 * NCH)

        @block.tensor
        def _(pe):
            def front_transposes(j):
                pe.wait_ge(xn_ready, j + 1)
                pe.wait_ge(hT_ready, j)
                for k in range(KD):
                    mm = pe.transpose(wideT[:, k, :], xin[:, k * P:(k + 1) * P], ident)
                mm.then_inc(xnT_ps, 1)

            def project(j, first, last):
                for g in range(first, last):
                    col, bank, written, reader, same = ITEMS[g // 4]
                    if g == 0:
                        pe.wait_ge(hT_ready, j + 1)
                    if g % 4 == 0:
                        pe.wait_ge(reader, j + same)
                    for k in range(KD):
                        mm = pe.matmul(pj[bank][:, g % 4, :], t.win[:, k, col + (g % 4) * P:col + (g % 4 + 1) * P],
                                       hT[:, k, :], start=(k == 0), stop=(k == KD - 1))
                    if g % 4 == 3:
                        mm.then_inc(written, 1)

            def project_z(j):
                pe.wait_ge(k_evac, j + 1)
                for k in range(KD):
                    mm = pe.matmul(pj[0][:].rearrange("p a b -> p (a b)"), hT[:, k, :], t.win[:, k, COL_Z:COL_Z + DNW],
                                   start=(k == 0), stop=(k == KD - 1))
                mm.then_inc(z_ps, 1)
                pe.wait_ge(lnr_var, j)
                for k in range(KD):
                    mm = pe.matmul(m_ba, hT[:, k, :], t.win[:, k, COL_BA:COL_BA + 2 * HEADS],
                                   start=(k == 0), stop=(k == KD - 1))
                mm.then_inc(ba_ps, 1)

            def decays(j):
                pe.wait_ge(gU_ready, j + 1)
                pe.wait_ge(oT_ready, j)
                pe.matmul(b7[:], t.cst[:, C_LS, :], gU[:], start=True, stop=True).then_inc(dec_ps, 1)
                pe.matmul(m_gate[:, 0:4], t.cst[:, C_UI, :], g4, start=True, stop=True)
                pe.matmul(m_gate[:, 4:8], t.cst[:, C_LS, :], g4, start=True, stop=True)
                pe.matmul(m_gate[:, 8:12], t.cst[:, C_ONE, :], g4, start=True, stop=True).then_inc(gates_ps, 1)

            def keys(i):
                pe.wait_ge(qkv_act, i + 1)
                pe.wait_ge(S_ready, i)
                pe.wait_ge(o_step, 2 * i)
                for h in range(HEADS):
                    pe.transpose(b5[:, h, :], qkvT[:, HEADS + h, :], ident)
                for h in range(HEADS):
                    mm = pe.transpose(b6[:, h, :], qkvT[:, 2 * HEADS + h, :], ident)
                mm.then_inc(kv_ps, 1)
                pe.wait_ge(qk_sq, i + 1)
                pe.wait_ge(lg_ready, i)
                for h in range(2 * HEADS):
                    mm = pe.matmul(m_ssq[:, h:h + 1], sq[:, h, :], t.cst[:, C_ONE, 0:1], start=True, stop=True)
                mm.then_inc(ssq_ps, 1)

            def ln_mean(i):
                pe.wait_ge(cf_tap, CFT * (i + 1))
                pe.wait_ge(ssn_ready, i + 1)
                for g in range(CFG):
                    mm = pe.matmul(m_mean, t.cst[:, C_ONE, :], cvf[:, g, :], start=(g == 0), stop=(g == CFG - 1))
                mm.then_inc(mean_ps, 1)

            def ln_var(i):
                pe.wait_ge(xc_sq, i + 1)
                for g in range(CFG):
                    mm = pe.matmul(m_var, t.cst[:, C_ONE, :], lnsq[:, g, :], start=(g == 0), stop=(g == CFG - 1))
                mm.then_inc(var_ps, 1)

            def scores(i):
                pe.wait_ge(khatT_ready, i + 1)
                pe.wait_ge(bv_ready, i + 1)
                for h in range(HEADS):
                    mm = pe.matmul(b6[:, h, :], khatT[:, h, :], khatT[:, h, :], start=True, stop=True)
                mm.then_inc(kk_ps, 1)
                pe.wait_ge(dec_exp, i + 1)
                for h in range(HEADS):
                    mm = pe.matmul(b7[:, h, :], khatT[:, h, :], qkvT[:, h, :], start=True, stop=True)
                mm.then_inc(attn_ps, 1)

            def level_p(i, l):
                pe.wait_ge(mask_done, i * LEVELS + l + 1)
                if l > 0:
                    pe.wait_ge(t_ready, i * (LEVELS - 1) + l)
                else:
                    pe.wait_ge(khatT_ready, i + 1)
                for h in range(HEADS):
                    mm = pe.matmul(b5[:, h, :], Kl[l % 2][:, h, :], ident if l == 0 else T[:, h, :], start=True, stop=True)
                mm.then_inc(p1_ps, 1)

            def level_tn(i, l):
                pe.wait_ge(p_ready, i * LEVELS + l + 1)
                if l == 0:
                    pe.wait_ge(attnT_ready, i + 1)
                else:
                    pe.wait_ge(n_ready, i * LEVELS + l)
                if l < LEVELS - 1:
                    for h in range(HEADS):
                        mm = pe.matmul(b6[:, h, :], ident if l == 0 else N[:, h, :], Pm[:, h, :], start=True, stop=True)
                    mm.then_inc(tp_ps, 1)
                for h in range(HEADS):
                    mm = pe.matmul(b7[:, h, :], Pm[:, h, :], ident if l == 0 else N[:, h, :], start=True, stop=True)
                mm.then_inc(pn_ps, 1)

            def scan(i, j):
                pe.wait_ge(n_ready, LEVELS * (i + 1))
                pe.wait_ge(kw_ready, i + 1)
                for h in range(HEADS):
                    mm = pe.matmul(b5[:, h, :], kw[:, h, :], N[:, h, :], start=True, stop=True)
                mm.then_inc(wT_ps, 1)
                for h in range(HEADS):
                    mm = pe.matmul(b7[:, h, :], qkvT[:, h, :], S[:, h, :], start=True, stop=True)
                mm.then_inc(oS_ps, 1)
                pe.wait_ge(nwT_ready, i + 1)
                for h in range(HEADS):
                    pe.matmul(b6[:, h, :], N[:, h, :], bv[:, h, :], start=True, stop=False)
                    mm = pe.matmul(b6[:, h, :], nwT[:, h, :], S[:, h, :], start=False, stop=True)
                mm.then_inc(vn_ps, 1)
                pe.wait_ge(vn_ready, i + 1)
                pe.wait_ge(kdec_ready, i + 1)
                for h in range(HEADS):
                    mm = pe.matmul(b6[:, h, :], khat[:, h, :], vn[:, h, :], start=True, stop=True)
                mm.then_inc(dS_ps, 1)
                for h in range(HEADS):
                    mm = pe.matmul(b5[:, h, :], attnT[:, h, :], vn[:, h, :], start=True, stop=True)
                mm.then_inc(oa_ps, 1)

            def head_transposes(i):
                pe.wait_ge(o_gated, i + 1)
                for h in range(HEADS):
                    mm = pe.transpose(b7[:, h, :], o1[:, h, :], ident)
                mm.then_inc(oT_ps, 1)

            def project_out(i, fronts):
                pe.wait_ge(hT_ready, fronts)
                pe.wait_ge(cf_ready, i + 1)
                pe.wait_ge(oT_ready, i + 1)
                for half in range(2):
                    for k in range(KD):
                        mm = pe.matmul(wide[:, half * 512:(half + 1) * 512], mixT[:, k, :],
                                       t.wout[:, k, half * 512:(half + 1) * 512], start=(k == 0), stop=(k == KD - 1))
                mm.then_inc(mix_ps, 1)

            def router(i, fronts):
                pe.wait_ge(h2n_ready, i + 1)
                hv = h2n[:].rearrange("p (q k) -> p k q", k=KD)
                for k in range(KD):
                    mm = pe.transpose(wideT[:, k, :], hv[:, k, :], ident)
                mm.then_inc(h2T_ps, 1)
                pe.wait_ge(h2T_ready, i + 1)
                pe.wait_ge(gates_exp, fronts)
                for k in range(KD):
                    mm = pe.matmul(m_lg, mixT[:, k, :], t.wr[:, k, :], start=(k == 0), stop=(k == KD - 1))
                mm.then_inc(lg_ps, 1)

            pe.wait_ge(consts_set, 1)
            front_transposes(0)
            project(0, 0, 20)
            project_z(0)
            decays(0)
            with pe.Fori(0, NCH - 1) as i:
                j = i + 1
                keys(i)
                pe.wait_ge(h2T_ready, i)
                front_transposes(j)
                pe.wait_ge(khat_ready, i + 1)
                for h in range(HEADS):
                    mm = pe.transpose(b5[:, h, :], khat[:, h, :], ident)
                mm.then_inc(khatT_ps, 1)
                ln_mean(i)
                project(j, 0, 4)
                scores(i)
                ln_var(i)
                for l in range(LEVELS):
                    level_p(i, l)
                    project(j, 4 + (16 * (2 * l)) // 14, 4 + (16 * (2 * l + 1)) // 14)
                    level_tn(i, l)
                    project(j, 4 + (16 * (2 * l + 1)) // 14, 4 + (16 * (2 * l + 2)) // 14)
                scan(i, j)
                project_z(j)
                head_transposes(i)
                project_out(i, j + 1)
                decays(j)
                router(i, j + 1)
            i = NCH - 1
            keys(i)
            pe.wait_ge(khat_ready, i + 1)
            for h in range(HEADS):
                mm = pe.transpose(b5[:, h, :], khat[:, h, :], ident)
            mm.then_inc(khatT_ps, 1)
            ln_mean(i)
            scores(i)
            ln_var(i)
            for l in range(LEVELS):
                level_p(i, l)
                level_tn(i, l)
            scan(i, i)
            head_transposes(i)
            project_out(i, NCH)
            router(i, NCH)

        @block.scalar
        def _(act):
            def front_ss(j):
                act.wait_ge(x_loaded, 16 * (j + 1))
                act.wait_ge(x_rstd, j)
                act.activation(junk[:], xin[:], ACT.Square, accum_out=ss0).then_inc(x_ss, 1)

            def front_hT(j):
                act.wait_ge(xnT_ps, j + 1)
                act.wait_ge(ba_ps, j)
                for k in range(KD):
                    ins = act.activation(hT[:, k, :], wideT[:, k, :], ACT.Identity, bias=t.B1[:, k:k + 1],
                                         scale=t.A1[:, k:k + 1])
                ins.then_inc(hT_ready, 1)

            def front_glu(j):
                act.wait_ge(cfa_ps, j + 1)
                act.wait_ge(halo_cf, j + 1)
                for g in range(CFG):
                    ins = act.activation(cfpre[:, g, CFT - 1:], pj[1][:, g, :], ACT.Identity, bias=t.halfb[:, g:g + 1], scale=0.5)
                ins.then_inc(cfa_evac, 1)
                act.wait_ge(cfb_ps, j + 1)
                act.wait_ge(glu_done, j)
                for g in range(CFG):
                    ins = act.activation(glut[:, g, :], pj[0][:, g, :], ACT.Tanh,
                                         bias=t.halfb[:, CFG + g:CFG + g + 1], scale=0.5)
                ins.then_inc(cfb_evac, 1)

            def front_qkv(j, n, written, evac):
                act.wait_ge(written, j + 1)
                if n == 0:
                    act.wait_ge(halo_dn, j + 1)
                bank = pj[1 - n % 2]
                act.copy(pre[:, 4 * n:4 * n + 4, DNT - 1:], bank[:]).then_inc(evac, 1)

            def front_z(j):
                act.wait_ge(z_ps, j + 1)
                act.wait_ge(o_gated, j)
                act.activation(zg[:], pj[0][:], ACT.Silu).then_inc(z_evac, 1)

            def front_gates(j):
                act.wait_ge(ba_neg, j + 1)
                act.wait_ge(beta_den, j)
                act.activation(e8, en, ACT.Exp).then_inc(ba_exp, 1)
                act.wait_ge(ba_exp, j + 1)
                act.activation(l4, e8[:, 4:8], ACT.Ln, bias=1.0).then_inc(ba_ln, 1)

            def front_decays(j):
                act.wait_ge(dec_ps, j + 1)
                act.wait_ge(attnT_ready, j)
                act.activation(EU[:], b7[:], ACT.Exp).then_inc(dec_exp, 1)
                act.wait_ge(gates_ps, j + 1)
                act.wait_ge(S_decayed, j)
                act.wait_ge(o_step, 2 * j)
                act.activation(ex, m_gate, ACT.Exp).then_inc(gates_exp, 1)

            def qkv(i):
                act.wait_ge(dn_tap, 12 * (i + 1))
                act.wait_ge(oS_ps, i)
                act.activation(qkvT[:], cv[:], ACT.Silu).then_inc(qkv_act, 1)
                act.wait_ge(qkv_act, i + 1)
                act.wait_ge(h2n_out, 16 * i)
                act.wait_ge(h2T_ps, i)
                act.activation(sq[:], qkvT[:, 0:2 * HEADS, :], ACT.Square).then_inc(qk_sq, 1)

            def khat_evac(i):
                act.wait_ge(khatT_ps, i + 1)
                act.copy(khatT[:], b5[:]).then_inc(khatT_ready, 1)

            def ln_square(i):
                act.wait_ge(xc_ready, i + 1)
                act.wait_ge(ssq_ps, i + 1)
                act.activation(lnsq, xc[:], ACT.Square).then_inc(xc_sq, 1)

            def ln_act(i):
                act.wait_ge(cfn_ready, i + 1)
                act.wait_ge(lg_ps, i)
                for g in range(CFG):
                    ins = act.activation(mixT[:, HEADS + g, :], xc[:, g, :], ACT.Silu,
                                         bias=t.chp[:, CH_LNB + g:CH_LNB + g + 1],
                                         scale=t.chp[:, CH_LNW + g:CH_LNW + g + 1])
                ins.then_inc(cf_ready, 1)

            def scan(i):
                act.wait_ge(wT_ps, i + 1)
                act.copy(nwT[:], b5[:]).then_inc(nwT_ready, 1)
                act.wait_ge(vn_ps, i + 1)
                act.copy(vn[:], b6[:]).then_inc(vn_ready, 1)

            def heads(i):
                act.wait_ge(oT_ps, i + 1)
                act.copy(mixT[:, 0:HEADS, :], b7[:]).then_inc(oT_ready, 1)

            def post(i):
                act.wait_ge(mix_ps, i + 1)
                act.activation(junk[:], wide[:], ACT.Square, accum_out=ss1).then_inc(mix_ss, 1)
                act.wait_ge(x1_ready, i + 1)
                act.activation(junk[:], x1[:], ACT.Square, accum_out=ss2).then_inc(x1_ss, 1)

            def h2(i):
                act.wait_ge(h2T_ps, i + 1)
                for k in range(KD):
                    ins = act.activation(mixT[:, k, :], wideT[:, k, :], ACT.Identity, bias=t.B2[:, k:k + 1],
                                         scale=t.A2[:, k:k + 1])
                ins.then_inc(h2T_ready, 1)

            front_ss(0)
            front_hT(0)
            front_glu(0)
            front_qkv(0, 0, q_ps, q_evac)
            front_qkv(0, 1, k_ps, k_evac)
            front_qkv(0, 2, v_ps, v_evac)
            front_z(0)
            front_gates(0)
            front_decays(0)
            with act.Fori(0, NCH - 1) as i:
                j = i + 1
                qkv(i)
                front_ss(j)
                front_hT(j)
                khat_evac(i)
                ln_square(i)
                front_glu(j)
                ln_act(i)
                front_qkv(j, 0, q_ps, q_evac)
                front_qkv(j, 1, k_ps, k_evac)
                front_qkv(j, 2, v_ps, v_evac)
                scan(i)
                front_z(j)
                heads(i)
                front_gates(j)
                post(i)
                front_decays(j)
                h2(i)
            i = NCH - 1
            qkv(i)
            khat_evac(i)
            ln_square(i)
            ln_act(i)
            scan(i)
            heads(i)
            post(i)
            h2(i)

        @block.gpsimd
        def _(pool):
            def rsqrt_row(src, mid, dst, after, var, done, j):
                pool.wait_ge(after, j + 1)
                pool.tensor_tensor(mid, src, eps_d, ALU.add).then_inc(var, 1)
                pool.wait_ge(var, j + 1)
                pool.tensor_tensor(dst, mid, hp[:, 0:1], ALU.pow).then_inc(done, 1)

            def front_rstd(j):
                pool.wait_ge(xn_ready, j)
                rsqrt_row(ss0, v0, rs0, x_ss, x_var, x_rstd, j)

            def front_z(j):
                pool.wait_ge(z_evac, j + 1)
                pool.tensor_tensor(zg[:], zg[:], over_heads(t.dnn[:], HEADS), ALU.mult).then_inc(z_ready, 1)

            def front_gU(j):
                pool.wait_ge(g_ready, j + 1)
                pool.wait_ge(p1_ps, LEVELS * j)
                pool.tensor_tensor(gU[:], over_heads(t.cst[:, C_UI, :], HEADS), over_cols(g4, P),
                                   ALU.mult).then_inc(gU_ready, 1)

            def front_EU(j):
                pool.wait_ge(dec_exp, j + 1)
                pool.tensor_tensor(EU[:], EU[:], over_heads(t.cst[:, C_UI, :], HEADS), ALU.mult).then_inc(EU_ready, 1)

            def keys(i):
                pool.wait_ge(ssn_ready, i + 1)
                pool.wait_ge(o_rs, i)
                pool.tensor_tensor(rqk, ssn, hp[:, 0:8], ALU.pow).then_inc(rqk_ready, 1)
                pool.wait_ge(khat_ready, i + 1)
                pool.wait_ge(nbe_ready, i + 1)
                pool.tensor_tensor(kw[:], khat[:], over_cols(nbe, P), ALU.mult).then_inc(kw_ready, 1)

            def key_decay(i):
                pool.wait_ge(khatT_ps, i + 1)
                pool.wait_ge(kw_ready, i + 1)
                pool.tensor_tensor(khat[:], khat[:], over_cols(ex[:, 4:8], P), ALU.mult).then_inc(kdec_ready, 1)

            def mask(i, l):
                if l == 0:
                    pool.wait_ge(KT_ready, i + 1)
                    pool.wait_ge(vn_ps, i)
                else:
                    pool.wait_ge(p1_ps, i * LEVELS + max(l - 1, 0))
                pool.tensor_tensor(Kl[l % 2][:], KT[:], over_heads(t.cst[:, C_LV + l, :], HEADS),
                                   ALU.mult).then_inc(mask_done, 1)

            def ln_rstd(i):
                pool.wait_ge(lnr_var, i + 1)
                pool.tensor_tensor(lnr[:], lnr[:], hp[:], ALU.pow).then_inc(lnr_ready, 1)

            def state(i):
                pool.wait_ge(vn_ps, i + 1)
                pool.wait_ge(oS_ps, i + 1)
                pool.tensor_tensor(S[:], S[:], over_cols(ex[:, 8:12], P), ALU.mult).then_inc(S_decayed, 1)

            def head_rstd(i):
                pool.wait_ge(o_ss, i + 1)
                step = 4 * i
                pool.tensor_tensor(scr[:, 0:4], rqk[:, 0:4], rqk[:, 0:4], ALU.mult).then_inc(pstep, 1)
                pool.wait_ge(pstep, step + 1)
                pool.tensor_tensor(scr[:, 4:8], scr[:, 0:4], oss, ALU.mult).then_inc(pstep, 1)
                pool.wait_ge(pstep, step + 2)
                pool.tensor_tensor(scr[:, 8:12], scr[:, 4:8], eps_hd2, ALU.add).then_inc(pstep, 1)
                pool.wait_ge(pstep, step + 3)
                pool.tensor_tensor(scr[:, 12:16], scr[:, 8:12], hp[:, 0:4], ALU.pow).then_inc(pstep, 1)
                pool.wait_ge(pstep, step + 4)
                pool.tensor_tensor(orr, scr[:, 12:16], rqk[:, 0:4], ALU.mult).then_inc(o_rs, 1)

            pool.memset(hp[:], -0.5)
            pool.memset(eps_d, D * EPS)
            pool.memset(eps_hd2, HD * HD * EPS)
            pool.memset(S[:], 0.0)
            pool.memset(pre[:, :, 0:DNT - 1], 0.0)
            pool.memset(cfpre[:, :, 0:CFT - 1], 0.0).then_inc(consts_set, 1)
            pool.wait_ge(consts_set, 1)
            front_rstd(0)
            front_z(0)
            front_gU(0)
            front_EU(0)
            with pool.Fori(0, NCH - 1) as i:
                j = i + 1
                front_rstd(j)
                keys(i)
                key_decay(i)
                mask(i, 0)
                mask(i, 1)
                ln_rstd(i)
                for l in range(2, LEVELS):
                    mask(i, l)
                state(i)
                head_rstd(i)
                front_z(j)
                front_gU(j)
                rsqrt_row(ss1, v1, rs1, mix_ss, mix_var, mix_rstd, i)
                rsqrt_row(ss2, v2, rs2, x1_ss, x1_var, x1_rstd, i)
                front_EU(j)
            i = NCH - 1
            keys(i)
            key_decay(i)
            mask(i, 0)
            mask(i, 1)
            ln_rstd(i)
            for l in range(2, LEVELS):
                mask(i, l)
            state(i)
            head_rstd(i)
            rsqrt_row(ss1, v1, rs1, mix_ss, mix_var, mix_rstd, i)
            rsqrt_row(ss2, v2, rs2, x1_ss, x1_var, x1_rstd, i)

        @block.vector
        def _(dve):
            def front_xn(j):
                dve.wait_ge(x_rstd, j + 1)
                dve.wait_ge(x_ss, j + 1)
                dve.tensor_scalar(xin[:], xin[:], rs0, ROOT_D, ALU.mult, ALU.mult).then_inc(xn_ready, 1)

            def front_halo(j):
                if isinstance(j, int):
                    dve.wait_ge(consts_set, 1)
                    dve.engine_nop().then_inc(halo_dn, 1)
                    dve.engine_nop().then_inc(halo_cf, 1)
                else:
                    dve.wait_ge(v_evac, j)
                    dve.wait_ge(dn_tap, 12 * j)
                    dve.tensor_copy(pre[:, :, 0:DNT - 1], pre[:, :, P:P + DNT - 1]).then_inc(halo_dn, 1)
                    dve.wait_ge(cf_tap, CFT * j)
                    dve.tensor_copy(cfpre[:, :, 0:CFT - 1], cfpre[:, :, P:P + CFT - 1]).then_inc(halo_cf, 1)

            def front_glu(j):
                dve.wait_ge(cfa_evac, j + 1)
                dve.wait_ge(cfb_evac, j + 1)
                dve.wait_ge(halo_cf, j + 1)
                new = cfpre[:, :, CFT - 1:]
                dve.scalar_tensor_tensor(new, glut[:], 1.0, new, ALU.add, ALU.mult).then_inc(glu_done, 1)

            def cf_rounds(j, first, last):
                for r in range(first, last):
                    if r == 0:
                        dve.wait_ge(glu_done, j + 1)
                        dve.wait_ge(mean_ps, j)
                        dve.wait_ge(xc_ready, j)
                    else:
                        dve.wait_ge(cf_tap, j * CFT + r)
                    for g in range(CFG):
                        w = t.chp[:, CH_CFW + g * CFT + r:CH_CFW + g * CFT + r + 1]
                        src = cfpre[:, g, r:r + P]
                        if r == 0:
                            ins = dve.tensor_scalar(cvf[:, g, :], src, w, t.chp[:, CH_DWB + g:CH_DWB + g + 1],
                                                    ALU.mult, ALU.add)
                        else:
                            ins = dve.scalar_tensor_tensor(cvf[:, g, :], src, w, cvf[:, g, :], ALU.mult, ALU.add)
                    ins.then_inc(cf_tap, 1)

            def dn_conv(j, n, evac):
                dve.wait_ge(evac, j + 1)
                if n == 0:
                    dve.wait_ge(qkv_act, j)
                    dve.wait_ge(halo_dn, j + 1)
                for r in range(DNT):
                    if r > 0:
                        dve.wait_ge(dn_tap, j * 12 + n * DNT + r)
                    for g in range(4 * n, 4 * n + 4):
                        w = t.chp[:, CH_DNW + g * DNT + r:CH_DNW + g * DNT + r + 1]
                        src = pre[:, g, r:r + P]
                        if r == 0:
                            ins = dve.tensor_scalar(cv[:, g, :], src, w, None, ALU.mult)
                        else:
                            ins = dve.scalar_tensor_tensor(cv[:, g, :], src, w, cv[:, g, :], ALU.mult, ALU.add)
                    ins.then_inc(dn_tap, 1)

            def front_ba(j):
                dve.wait_ge(ba_ps, j + 1)
                dve.wait_ge(ba_exp, j)
                dve.tensor_tensor(bal, m_ba, t.babias[:], ALU.add).then_inc(ba_biased, 1)
                dve.wait_ge(ba_biased, j + 1)
                dve.tensor_scalar(en[:, 0:4], bal[:, 0:4], -1.0, None, ALU.mult)
                dve.scalar_tensor_tensor(en[:, 4:8], bal[:, 4:8], -1.0, bal[:, 4:8], ALU.mult, ALU.min).then_inc(ba_neg, 1)

            def front_g(j):
                dve.wait_ge(ba_exp, j + 1)
                dve.tensor_scalar(beta, e8[:, 0:4], 1.0, None, ALU.add).then_inc(beta_den, 1)
                dve.wait_ge(ba_ln, j + 1)
                dve.scalar_tensor_tensor(sp4, bal[:, 4:8], 0.0, l4, ALU.max, ALU.add).then_inc(softplus, 1)
                dve.wait_ge(beta_den, j + 1)
                dve.reciprocal(beta, beta)
                dve.wait_ge(softplus, j + 1)
                dve.wait_ge(gates_ps, j)
                dve.tensor_tensor(g4, sp4, t.nega[:], ALU.mult).then_inc(g_ready, 1)

            def front_nbe(j):
                dve.wait_ge(gates_exp, j + 1)
                dve.wait_ge(g_ready, j + 1)
                dve.scalar_tensor_tensor(nbe, beta, -1.0, ex[:, 0:4], ALU.mult, ALU.mult).then_inc(nbe_ready, 1)

            def keys(i):
                dve.wait_ge(ssq_ps, i + 1)
                dve.tensor_scalar(ssn, m_ssq, EPS, None, ALU.add).then_inc(ssn_ready, 1)

            def khats(i):
                dve.wait_ge(kv_ps, i + 1)
                dve.wait_ge(g_ready, i + 1)
                dve.tensor_tensor(bv[:], b6[:], over_cols(beta, P), ALU.mult).then_inc(bv_ready, 1)
                dve.wait_ge(rqk_ready, i + 1)
                dve.wait_ge(dS_ps, i)
                dve.tensor_tensor(khat[:], b5[:], over_cols(rqk[:, 4:8], P), ALU.mult).then_inc(khat_ready, 1)

            def ln_center(i):
                dve.wait_ge(mean_ps, i + 1)
                dve.wait_ge(cf_ready, i)
                dve.scalar_tensor_tensor(xc[:], over_heads(m_mean, CFG), -1.0 / CFW, cvf[:], ALU.mult,
                                         ALU.add).then_inc(xc_ready, 1)

            def ln_eps(i):
                dve.wait_ge(var_ps, i + 1)
                dve.wait_ge(cfn_ready, i)
                dve.tensor_scalar(lnr[:], m_var, 1.0 / CFW, EPS, ALU.mult, ALU.add).then_inc(lnr_var, 1)

            def ln_scale(i):
                dve.wait_ge(lnr_ready, i + 1)
                dve.wait_ge(xc_sq, i + 1)
                dve.tensor_tensor(xc[:], xc[:], over_heads(lnr[:], CFG), ALU.mult).then_inc(cfn_ready, 1)

            def scores(i):
                dve.wait_ge(kk_ps, i + 1)
                dve.wait_ge(EU_ready, i + 1)
                dve.wait_ge(oT_ps, i)
                dve.tensor_tensor(KT[:], b6[:], EU[:], ALU.mult).then_inc(KT_ready, 1)
                dve.wait_ge(attn_ps, i + 1)
                dve.wait_ge(oa_ps, i)
                dve.tensor_tensor(attnT[:], b7[:], EU[:], ALU.mult).then_inc(attnT_ready, 1)

            def level_p(i, l):
                dve.wait_ge(p1_ps, i * LEVELS + l + 1)
                if l == 0:
                    dve.wait_ge(dS_ps, i)
                    dve.wait_ge(oa_ps, i)
                else:
                    dve.wait_ge(pn_ps, i * LEVELS + l)
                dve.tensor_tensor(Pm[:], b5[:], over_cols(beta, P), ALU.mult).then_inc(p_ready, 1)

            def level_t(i, l):
                if l < LEVELS - 1:
                    dve.wait_ge(tp_ps, i * (LEVELS - 1) + l + 1)
                    if l == 0:
                        dve.wait_ge(o_ss, i)
                    else:
                        dve.wait_ge(t_ready, i * (LEVELS - 1) + l)
                    dve.tensor_tensor(T[:], over_heads(ident, HEADS) if l == 0 else T[:], b6[:],
                                      ALU.subtract).then_inc(t_ready, 1)

            def level_n(i, l):
                dve.wait_ge(pn_ps, i * LEVELS + l + 1)
                if l == 0:
                    dve.wait_ge(vn_ps, i)
                else:
                    dve.wait_ge(n_ready, i * LEVELS + l)
                dve.tensor_tensor(N[:], over_heads(ident, HEADS) if l == 0 else N[:], b7[:],
                                  ALU.subtract).then_inc(n_ready, 1)

            def output(i):
                dve.wait_ge(oS_ps, i + 1)
                dve.wait_ge(mask_done, (i + 1) * LEVELS)
                dve.wait_ge(gates_exp, i + 1)
                dve.tensor_tensor(o1[:], b7[:], over_cols(ex[:, 0:4], P), ALU.mult).then_inc(o_step, 1)
                dve.wait_ge(dS_ps, i + 1)
                dve.wait_ge(S_decayed, i + 1)
                dve.tensor_tensor(S[:], S[:], b6[:], ALU.add).then_inc(S_ready, 1)
                dve.wait_ge(oa_ps, i + 1)
                dve.wait_ge(o_step, 2 * i + 1)
                dve.tensor_tensor(o1[:], o1[:], b5[:], ALU.add).then_inc(o_step, 1)
                dve.wait_ge(o_step, 2 * i + 2)
                dve.wait_ge(p1_ps, (i + 1) * LEVELS)
                dve.tensor_tensor(o2[:], o1[:], o1[:], ALU.mult).then_inc(o2_ready, 1)
                dve.wait_ge(o2_ready, i + 1)
                dve.tensor_reduce(oss, o2[:], AXX, ALU.add).then_inc(o_ss, 1)

            def gate(i):
                dve.wait_ge(o_rs, i + 1)
                dve.tensor_tensor(o1[:], o1[:], over_cols(orr, P), ALU.mult).then_inc(o_scaled, 1)
                dve.wait_ge(z_ready, i + 1)
                dve.wait_ge(o_scaled, i + 1)
                dve.tensor_tensor(o1[:], o1[:], zg[:], ALU.mult).then_inc(o_gated, 1)

            def post(i):
                dve.wait_ge(mix_rstd, i + 1)
                dve.wait_ge(xc_sq, i + 1)
                dve.wait_ge(var_ps, i + 1)
                dve.scalar_tensor_tensor(h2n[:], wide[:], rs1, t.G1[:], ALU.mult, ALU.mult).then_inc(mix_normed, 1)
                dve.wait_ge(mix_normed, i + 1)
                dve.wait_ge(xr_loaded, 16 * (i + 1))
                dve.tensor_tensor(x1[:], x1[:], h2n[:], ALU.add).then_inc(x1_ready, 1)

            def h2(i):
                dve.wait_ge(x1_rstd, i + 1)
                dve.wait_ge(x1_ready, i + 1)
                dve.tensor_scalar(h2n[:], x1[:], rs2, ROOT_D, ALU.mult, ALU.mult).then_inc(h2n_ready, 1)

            def logits(i):
                dve.wait_ge(lg_ps, i + 1)
                dve.wait_ge(lg_out, 16 * i)
                dve.tensor_tensor(lgs[:], m_lg, t.rbias[:], ALU.add).then_inc(lg_ready, 1)

            o2_ready, o_scaled = sem("o2_ready"), sem("o_scaled")

            front_xn(0)
            front_halo(0)
            front_glu(0)
            cf_rounds(0, 0, CFT)
            dn_conv(0, 0, q_evac)
            dn_conv(0, 1, k_evac)
            dn_conv(0, 2, v_evac)
            front_ba(0)
            front_g(0)
            front_nbe(0)
            with dve.Fori(0, NCH - 1) as i:
                j = i + 1
                keys(i)
                front_xn(j)
                khats(i)
                ln_center(i)
                front_halo(j)
                scores(i)
                ln_eps(i)
                level_p(i, 0)
                level_t(i, 0)
                level_n(i, 0)
                ln_scale(i)
                level_p(i, 1)
                level_t(i, 1)
                level_n(i, 1)
                front_glu(j)
                for l in range(2, LEVELS):
                    r = 6 * (l - 2)
                    level_p(i, l)
                    cf_rounds(j, r, r + 3)
                    level_t(i, l)
                    level_n(i, l)
                    cf_rounds(j, r + 3, r + 6)
                output(i)
                cf_rounds(j, 30, CFT)
                gate(i)
                dn_conv(j, 0, q_evac)
                dn_conv(j, 1, k_evac)
                front_ba(j)
                front_g(j)
                post(i)
                h2(i)
                front_nbe(j)
                dn_conv(j, 2, v_evac)
                logits(i)
            i = NCH - 1
            keys(i)
            khats(i)
            ln_center(i)
            scores(i)
            ln_eps(i)
            for l in range(LEVELS):
                level_p(i, l)
                level_t(i, l)
                level_n(i, l)
                if l == 0:
                    ln_scale(i)
            output(i)
            gate(i)
            post(i)
            h2(i)
            logits(i)
    nc.clear_and_free_semaphores(sems)
    nc.all_engine_barrier()


def build_routing(nc, r, t, dram):
    with ExitStack() as own:
        def sb(name, shape, dt=F32):
            return own.enter_context(nc.sbuf_tensor(name, shape, dt))

        def sem(name):
            return t.ctx.enter_context(nc.semaphore(name))

        lg = sb("lg_all", [P, NCH, NR])
        ids0 = sb("ids0", [P, NCH, 2], I32)
        io8 = sb("io8", [P, 2, NG])
        iop = sb("iop", [P, 1])
        gm, gs, m1, m2, ix, ew, dk = (sb(n, [P, NCH]) for n in ("gm", "gs", "m1", "m2", "ix", "ew", "dk"))
        ge, eq, ohg, sel, oh1, oh2, sel2 = (sb(n, [P, NCH, NG]) for n in ("ge", "eq", "ohg", "sel", "oh1", "oh2", "sel2"))
        M1, M2, MM, CC, V = (sb(n, [P, NCH, NG, EPG]) for n in ("M1", "M2", "MM", "CC", "V"))
        tot, nb, pend, pst, pst128, cmp_, ne, cs, pe_ = (
            sb(n, [P, NE]) for n in ("tot", "nb", "pend", "pst", "pst128", "cmp", "ne", "cs", "pstart_is"))
        nbi = sb("nbi", [P, NE], I32)
        di, rowi = sb("di", [P, NCH], I32), sb("rowi", [P, NCH], I32)
        dest = sb("dest", [P, NCH, 2], U32)
        inf = sb("inf", [P, 4])
        seq, nne, qf = sb("seq", [P, 1]), sb("nne", [P, 1]), sb("qf", [P, 1])
        qi = sb("qi", [P, 1], I32)
        fill = sb("fill", [P, BLOCKS + 2], U32)
        rk = own.enter_context(nc.psum_tensor("rank_ps", [P, NCH * NE], F32))
        ip = own.enter_context(nc.psum_tensor("info_ps", [P, 512], F32))
        cn = own.enter_context(nc.psum_tensor("count_ps", [P, 512], F32))[:, 0:NE]
        loaded, step, shifted, gexp, need_e2, e2, m_ready, rank_ps, info_cols, info_ps = map(sem, (
            "route_in", "route_step", "group_shifted", "group_exp", "gap_ready", "gap_exp", "choices_ready",
            "rank_ps", "info_cols", "info_ps"))
        filled, dest_ready, scattered, table_in = map(sem, ("filled", "dest_ready", "scattered", "table_in"))
        fill_set, ready = sem("fill_set"), sem("route_ready")

        block = own.enter_context(nc.Block())

        @block.sync
        def _(sp):
            sp.dma_start(lg[:], dram["lg"].rearrange("t p e -> p t e")).then_inc(loaded, 16)
            sp.dma_start(ids0[:], dram["ids"]).then_inc(loaded, 16)
            sp.dma_start(io8[:], dram["io8"]).then_inc(loaded, 16)
            sp.dma_start(iop[:], dram["iop"]).then_inc(loaded, 16)
            sp.wait_ge(fill_set, 1)
            sp.dma_start(dram["table"].rearrange("(p b) o -> p (b o)", p=P), fill[:]).then_inc(filled, 16)
            sp.wait_ge(scattered, 16 * 2 * NCH)
            sp.dma_start(r.ids[:], dram["table"].rearrange("(p b) o -> p (b o)", p=P)).then_inc(table_in, 16)
            sp.wait_ge(table_in, 16)

        @block.gpsimd
        def _(pool):
            pool.memset(fill[:], FREE_ROW).then_inc(fill_set, 1)
            pool.wait_ge(filled, 16)
            pool.wait_ge(dest_ready, 2)
            for n in range(NCH):
                for k in range(2):
                    pool.indirect_dma_start(
                        out=dram["table"], out_offset=bass.IndirectOffsetOnAxis(ap=dest[:, n, k:k + 1], axis=0),
                        in_=ids0[:, n, k:k + 1].bitcast(U32), in_offset=None).then_inc(scattered, 16)
            pool.wait_ge(scattered, 16 * 2 * NCH)

        @block.scalar
        def _(act):
            act.wait_ge(shifted, 1)
            act.activation(ge[:], ge[:], ACT.Exp).then_inc(gexp, 1)
            act.wait_ge(need_e2, 1)
            act.activation(ew[:], ew[:], ACT.Exp).then_inc(e2, 1)

        @block.tensor
        def _(pe):
            pe.wait_ge(m_ready, 1)
            mmv = MM[:].rearrange("p t g e -> p (t g e)")
            ccv = CC[:].rearrange("p t g e -> p (t g e)")
            pe.matmul(cn, t.cst[:, C_ONE, :], tot[:], start=True, stop=True).then_inc(rank_ps, 1)
            for half in range(2):
                c = slice(half * 512, half * 512 + 512)
                pe.matmul(rk[:, c], t.cst[:, C_US, :], mmv[:, c], start=True, stop=False)
                mm = pe.matmul(rk[:, c], t.cst[:, C_ONE, :], ccv[:, c], start=False, stop=True)
            mm.then_inc(rank_ps, 1)
            pe.wait_ge(info_cols, 1)
            for q in range(4):
                mm = pe.matmul(ip[0:1, q * P:(q + 1) * P], inf[:, q:q + 1], t.cst[:, C_ID, :], start=True, stop=True)
            mm.then_inc(info_ps, 1)

        @block.vector
        def _(dve):
            count = [0]

            def then(ins):
                count[0] += 1
                ins.then_inc(step, 1)
                dve.wait_ge(step, count[0])

            def onehot(values, top, out):
                then(dve.tensor_tensor(eq[:], values, over_cols(top, NG), ALU.is_equal))
                then(dve.scalar_tensor_tensor(eq[:], eq[:], -64.0, over_heads(io8[:, 1, :], NCH), ALU.mult, ALU.add))
                then(dve.tensor_reduce(ix[:], eq[:], AXX, ALU.min))
                then(dve.tensor_tensor(out, over_heads(io8[:, 0, :], NCH), over_cols(ix[:], NG), ALU.is_equal))

            dve.wait_ge(loaded, 64)
            G = lg[:, :, 0:NG]
            E = lg[:, :, NG:NR].rearrange("p t (g e) -> p t g e", g=NG)
            then(dve.tensor_reduce(gm[:], G, AXX, ALU.max))
            dve.tensor_tensor(ge[:], G, over_cols(gm[:], NG), ALU.subtract).then_inc(shifted, 1)
            onehot(G, gm[:], ohg[:])
            ohg4 = ohg[:].unsqueeze(3).to_broadcast([P, NCH, NG, EPG])
            then(dve.tensor_tensor(V[:], E, ohg4, ALU.mult))
            then(dve.tensor_reduce(sel[:], V[:].rearrange("p t g e -> p t e g"), AXX, ALU.add))
            then(dve.tensor_reduce(m1[:], sel[:], AXX, ALU.max))
            onehot(sel[:], m1[:], oh1[:])
            then(dve.scalar_tensor_tensor(sel2[:], oh1[:], -1e30, sel[:], ALU.mult, ALU.add))
            then(dve.tensor_reduce(m2[:], sel2[:], AXX, ALU.max))
            onehot(sel2[:], m2[:], oh2[:])
            dve.tensor_tensor(ew[:], m2[:], m1[:], ALU.subtract).then_inc(need_e2, 1)
            then(dve.tensor_tensor(M1[:], ohg4, oh1[:].unsqueeze(2).to_broadcast([P, NCH, NG, EPG]), ALU.mult))
            then(dve.tensor_tensor(M2[:], ohg4, oh2[:].unsqueeze(2).to_broadcast([P, NCH, NG, EPG]), ALU.mult))
            then(dve.tensor_tensor(MM[:], M1[:], M2[:], ALU.add))
            then(dve.memset(CC[:, 0], 0.0))
            for n in range(1, NCH):
                then(dve.tensor_tensor(CC[:, n], CC[:, n - 1], MM[:, n - 1], ALU.add))
            dve.tensor_tensor(tot[:].rearrange("p (g e) -> p g e", g=NG), CC[:, NCH - 1], MM[:, NCH - 1],
                              ALU.add).then_inc(m_ready, 1)
            dve.wait_ge(rank_ps, 1)
            then(dve.tensor_scalar(nbi[:], cn, float(P - 1), None, ALU.add))
            then(dve.tensor_scalar(nbi[:], nbi[:], 7, None, ALU.logical_shift_right))
            then(dve.tensor_copy(nb[:], nbi[:]))
            then(dve.tensor_tensor_scan(pend[:], t.cst[:, C_ONE, 0:NE], nb[:], 0.0, ALU.mult, ALU.add))
            then(dve.tensor_tensor(pst[:], pend[:], nb[:], ALU.subtract))
            then(dve.tensor_scalar(pst128[:], pst[:], float(P), None, ALU.mult))
            dve.wait_ge(rank_ps, 2)
            v3 = V[:].rearrange("p t g e -> p t (g e)")
            then(dve.tensor_tensor(v3, rk[:].rearrange("p (t e) -> p t e", t=NCH), over_heads(pst128[:], NCH), ALU.add))
            for k, M in enumerate((M1, M2)):
                then(dve.tensor_tensor(M[:], M[:], V[:], ALU.mult))
                then(dve.tensor_reduce(dk[:], M[:].rearrange("p t g e -> p t (g e)"), AXX, ALU.add))
                then(dve.tensor_copy(di[:], dk[:]))
                then(dve.tensor_scalar(rowi[:], di[:], P - 1, None, ALU.bitwise_and))
                then(dve.tensor_scalar(di[:], di[:], 7, None, ALU.logical_shift_right))
                dve.scalar_tensor_tensor(dest[:, :, k], rowi[:], float(BLOCKS + 2), di[:], ALU.mult,
                                         ALU.add).then_inc(dest_ready, 1)
                dve.wait_ge(dest_ready, k + 1)
            dve.wait_ge(gexp, 1)
            then(dve.tensor_reduce(gs[:], ge[:], AXX, ALU.add))
            dve.wait_ge(e2, 1)
            then(dve.scalar_tensor_tensor(gs[:], ew[:], 1.0, gs[:], ALU.add, ALU.mult))
            then(dve.reciprocal(r.wts[:, :, 0], gs[:]))
            then(dve.tensor_tensor(r.wts[:, :, 1], r.wts[:, :, 0], ew[:], ALU.mult))
            then(dve.tensor_scalar(ne[:], nb[:], 0.0, None, ALU.is_gt))
            then(dve.tensor_reduce(nne[:], ne[:], AXX, ALU.add))
            then(dve.tensor_scalar(cmp_[:], pend[:], iop[:], None, ALU.is_le))
            then(dve.tensor_reduce(inf[:, 0:1], cmp_[:], AXX, ALU.add))
            then(dve.tensor_scalar(inf[:, 0:1], inf[:, 0:1], float(NE - 1), None, ALU.min))
            then(dve.tensor_tensor(cs[:], cmp_[:], ne[:], ALU.mult))
            then(dve.tensor_reduce(seq[:], cs[:], AXX, ALU.add))
            then(dve.tensor_scalar(nne[:], nne[:], -1.0, None, ALU.add))
            then(dve.tensor_tensor(seq[:], seq[:], nne[:], ALU.min))
            then(dve.tensor_scalar(qi[:], seq[:], -1.0, 1.0 / SLOTS, ALU.add, ALU.mult))
            then(dve.tensor_copy(qf[:], qi[:]))
            then(dve.scalar_tensor_tensor(inf[:, 1:2], qf[:], -float(SLOTS), seq[:], ALU.mult, ALU.add))
            then(dve.tensor_scalar(pe_[:], pst[:], iop[:], None, ALU.is_equal))
            then(dve.tensor_tensor(pe_[:], pe_[:], ne[:], ALU.mult))
            then(dve.tensor_reduce(inf[:, 2:3], pe_[:], AXX, ALU.add))
            dve.tensor_copy(inf[:, 3:4], pend[:, NE - 1:NE]).then_inc(info_cols, 1)
            dve.wait_ge(info_ps, 1)
            then(dve.tensor_copy(r.info[0:1, 0:4 * P], ip[0:1, :]))
            then(dve.tensor_scalar(r.info[0:1, 4 * P:4 * P + 1], r.info[0:1, 3 * P:3 * P + 1], 1.0, None, ALU.add))
            then(dve.tensor_scalar(r.info[0:1, 4 * P:4 * P + 1], r.info[0:1, 4 * P:4 * P + 1], 1, None,
                                   ALU.logical_shift_right))
            dve.wait_ge(table_in, 16)
            dve.tensor_scalar(r.tok[:].bitcast(I32), r.ids[:].bitcast(I32), 1, None,
                              ALU.logical_shift_right).then_inc(ready, 1)
            dve.wait_ge(ready, 1)


def build_experts(nc, r, t, dram):
    with ExitStack() as own:
        def sb(name, shape, dt=F32):
            return own.enter_context(nc.sbuf_tensor(name, shape, dt))

        def sem(name):
            return t.ctx.enter_context(nc.semaphore(name))

        def two(make, name, *a):
            return [make(f"{name}{u}", *a) for u in range(2)]

        wgu = sb("wgu", [P, SLOTS * GU_COLS])
        wdn = sb("wdn", [P, SLOTS * DN_COLS])
        xg, xT = two(sb, "xg", [P, D]), two(sb, "xT", [P, KD, P])
        hs, hT = two(sb, "hid", [P, DE]), two(sb, "hidT", [P, KE, P])
        y = two(sb, "y", [P, D])
        gcol, scol = two(sb, "gather_rows", [P, 1], U32), two(sb, "scatter_rows", [P, 1], U32)
        gu = [own.enter_context(nc.psum_tensor(f"gu{u}_ps", [P, D], F32)) for u in range(2)]
        hp = [own.enter_context(nc.psum_tensor(f"hidT{u}_ps", [P, KE, P], F32)) for u in range(2)]
        yp = [own.enter_context(nc.psum_tensor(f"y{n}_ps", [P, 512], F32)) for n in range(2)]

        gu_in, dn_in = two(sem, "gate_up_in"), two(sem, "down_in")
        cleared = sem("xg_cleared")
        gcol_set, scol_set, x_in, y_out = (two(sem, n) for n in ("gather_rows_set", "scatter_rows_set", "x_in", "y_out"))
        xT_ps, xT_ready, gate_ps, up_ps, silu_done, hid_ready, hidT_ps, hidT_ready = (two(sem, n) for n in (
            "xT_ps", "xT_ready", "gate_ps", "up_ps", "silu_done", "hid_ready", "hidT_ps", "hidT_ready"))
        yh_ps, yh_read = sem("y_half_ps"), sem("y_half_read")
        y_ready = two(sem, "y_ready")
        ident = t.cst[:, C_ID, :]

        def pairs_of(eng):
            return eng.value_load(r.info[0:1, 4 * P:4 * P + 1], min_val=2 * SEQ // P // 2, max_val=BLOCKS // 2)

        block = own.enter_context(nc.Block())

        @block.sync
        def _(sp):
            pairs = pairs_of(sp)
            landed = [sp.alloc_register("gate_up_landed"), sp.alloc_register("down_landed")]

            def load(i, u):
                b = 2 * i + u
                e = sp.value_load(r.info[0:1, bass.ds(b, 1)], min_val=0, max_val=NE - 1)
                slot = sp.value_load(r.info[0:1, bass.ds(b + P, 1)], min_val=0, max_val=SLOTS - 1)
                new = sp.value_load(r.info[0:1, bass.ds(b + 2 * P, 1)], min_val=0, max_val=1)
                first = isinstance(i, int)
                if not first:
                    sp.reg_mul(landed[0], i, 32)
                    sp.reg_mul(landed[1], i, 16)
                    gu_landed, dn_landed = sp.snap(landed[0]), sp.snap(landed[1])
                    sp.wait_ge(up_ps[1 - u], i - 1 + u)
                    sp.wait_ge(gu_in[u], gu_landed)
                for m, w in enumerate(("w_gate", "w_up")):
                    sp.dma_start(wgu[:, bass.ds(slot * GU_COLS + m * KD * DE, KD * DE)],
                                 dram[w][bass.ds(e, 1)].rearrange("o (p k) f -> p (o k f)", p=P),
                                 cond=new).then_inc(gu_in[u], 16)
                if not first:
                    sp.wait_ge(yh_ps, 4 * i - 4 + 2 * u)
                    sp.wait_ge(dn_in[u], dn_landed)
                sp.dma_start(wdn[:, bass.ds(slot * DN_COLS, DN_COLS)],
                             dram["w_down"][bass.ds(e, 1)].rearrange("o (p k) d -> p (o k d)", p=P),
                             cond=new).then_inc(dn_in[u], 16)

            load(0, 0)
            load(0, 1)
            with sp.Fori(1, pairs) as i:
                load(i, 0)
                load(i, 1)

        @block.gpsimd
        def _(pool):
            pairs = pairs_of(pool)

            def gather(i, u):
                pool.wait_ge(x_in[u], 16 * i)
                pool.wait_ge(xT_ps[u], i)
                pool.tensor_copy(gcol[u][:], r.tok[:, bass.ds(2 * i + u, 1)]).then_inc(gcol_set[u], 1)
                pool.wait_ge(gcol_set[u], i + 1)
                pool.wait_ge(cleared, 1)
                pool.indirect_dma_start(out=xg[u][:], out_offset=None, in_=dram["h2"],
                                        in_offset=bass.IndirectOffsetOnAxis(ap=gcol[u][:], axis=0),
                                        bounds_check=i + (SEQ - 1 + u), oob_is_err=False).then_inc(x_in[u], 16)

            def scatter(i, u):
                pool.wait_ge(y_out[u], 16 * i)
                pool.tensor_copy(scol[u][:], r.ids[:, bass.ds(2 * i + u, 1)]).then_inc(scol_set[u], 1)
                pool.wait_ge(scol_set[u], i + 1)
                pool.wait_ge(y_ready[u], 2 * (i + 1))
                pool.wait_ge(cleared, 1)
                pool.indirect_dma_start(out=dram["y"], out_offset=bass.IndirectOffsetOnAxis(ap=scol[u][:], axis=0),
                                        in_=y[u][:], in_offset=None,
                                        bounds_check=i + (2 * SEQ - 1 + u), oob_is_err=False).then_inc(y_out[u], 16)

            pool.memset(xg[0][:], 0.0)
            pool.memset(xg[1][:], 0.0).then_inc(cleared, 1)
            pool.wait_ge(cleared, 1)
            gather(0, 0)
            gather(0, 1)
            with pool.Fori(0, pairs) as i:
                gather(i + 1, 0)
                gather(i + 1, 1)
                scatter(i, 0)
                scatter(i, 1)
            for u in range(2):
                pool.wait_ge(x_in[u], 16 * (pairs + 1))
                pool.wait_ge(y_out[u], 16 * pairs)

        @block.tensor
        def _(pe):
            pairs = pairs_of(pe)

            def x_transposes(i, u):
                pe.wait_ge(x_in[u], 16 * (i + 1))
                pe.wait_ge(hid_ready[u], i)
                xv = xg[u][:].rearrange("p (q k) -> p k q", k=KD)
                for k in range(KD):
                    mm = pe.transpose(gu[u][:, k * P:(k + 1) * P], xv[:, k, :], ident)
                mm.then_inc(xT_ps[u], 1)

            def gate_up(i, u, slot, m):
                if m == 0:
                    pe.wait_ge(gu_in[u], 32 * (i + 1))
                    pe.wait_ge(xT_ready[u], i + 1)
                for k in range(KD):
                    mm = pe.matmul(gu[u][:, m * DE:(m + 1) * DE], xT[u][:, k, :],
                                   wgu[:, bass.ds(slot * GU_COLS + (m * KD + k) * DE, DE)],
                                   start=(k == 0), stop=(k == KD - 1))
                mm.then_inc(up_ps[u] if m else gate_ps[u], 1)

            def hid_transposes(i, u):
                pe.wait_ge(hid_ready[u], i + 1)
                pe.wait_ge(hidT_ready[u], i)
                hv = hs[u][:].rearrange("p (q k) -> p k q", k=KE)
                for k in range(KE):
                    mm = pe.transpose(hp[u][:, k, :], hv[:, k, :], ident)
                mm.then_inc(hidT_ps[u], 1)

            def down(i, u, slot, half):
                if half == 0:
                    pe.wait_ge(dn_in[u], 16 * (i + 1))
                    pe.wait_ge(hidT_ready[u], i + 1)
                pe.wait_ge(yh_read, 4 * i + max(2 * u + half - 1, 0) if u or half else 4 * i)
                for k in range(KE):
                    mm = pe.matmul(yp[half][:], hT[u][:, k, :],
                                   wdn[:, bass.ds(slot * DN_COLS + k * D + half * 512, 512)],
                                   start=(k == 0), stop=(k == KE - 1))
                mm.then_inc(yh_ps, 1)

            x_transposes(0, 0)
            x_transposes(0, 1)
            with pe.Fori(0, pairs) as i:
                slots = [pe.value_load(r.info[0:1, bass.ds(2 * i + u + P, 1)], min_val=0, max_val=SLOTS - 1)
                         for u in range(2)]
                gate_up(i, 0, slots[0], 0)
                gate_up(i, 0, slots[0], 1)
                gate_up(i, 1, slots[1], 0)
                hid_transposes(i, 0)
                gate_up(i, 1, slots[1], 1)
                x_transposes(i + 1, 0)
                down(i, 0, slots[0], 0)
                hid_transposes(i, 1)
                x_transposes(i + 1, 1)
                down(i, 0, slots[0], 1)
                down(i, 1, slots[1], 0)
                down(i, 1, slots[1], 1)

        @block.scalar
        def _(act):
            pairs = pairs_of(act)

            def x_evac(i, u):
                act.wait_ge(xT_ps[u], i + 1)
                act.wait_ge(up_ps[u], i)
                for k in range(KD):
                    ins = act.activation(xT[u][:, k, :], gu[u][:, k * P:(k + 1) * P], ACT.Identity,
                                         bias=t.B2[:, k:k + 1], scale=t.A2[:, k:k + 1])
                ins.then_inc(xT_ready[u], 1)

            def silu(i, u):
                act.wait_ge(gate_ps[u], i + 1)
                act.wait_ge(hidT_ps[u], i)
                act.activation(hs[u][:], gu[u][:, 0:DE], ACT.Silu).then_inc(silu_done[u], 1)

            def hid_evac(i, u):
                act.wait_ge(hidT_ps[u], i + 1)
                act.wait_ge(yh_ps, 4 * i)
                act.copy(hT[u][:], hp[u][:]).then_inc(hidT_ready[u], 1)

            x_evac(0, 0)
            x_evac(0, 1)
            with act.Fori(0, pairs) as i:
                silu(i, 0)
                hid_evac(i, 0)
                silu(i, 1)
                x_evac(i + 1, 0)
                hid_evac(i, 1)
                x_evac(i + 1, 1)

        @block.vector
        def _(dve):
            pairs = pairs_of(dve)

            def hid(i, u):
                dve.wait_ge(up_ps[u], i + 1)
                dve.wait_ge(silu_done[u], i + 1)
                dve.tensor_tensor(hs[u][:], hs[u][:], gu[u][:, DE:2 * DE], ALU.mult).then_inc(hid_ready[u], 1)

            def y_evac(i, u, half):
                dve.wait_ge(yh_ps, 4 * i + 2 * u + half + 1)
                dve.wait_ge(y_out[u], 16 * i)
                dve.tensor_copy(y[u][:, half * 512:(half + 1) * 512], yp[half][:]).then_inc(yh_read, 1)
                if half:
                    dve.wait_ge(yh_read, 4 * i + 2 * u + 2)
                    dve.engine_nop().then_inc(y_ready[u], 2)

            with dve.Fori(0, pairs) as i:
                hid(i, 0)
                hid(i, 1)
                for u in range(2):
                    for half in range(2):
                        y_evac(i, u, half)


def build_combine(nc, r, t, dram):
    with ExitStack() as own:
        def sb(name, shape, dt=F32):
            return own.enter_context(nc.sbuf_tensor(name, shape, dt))

        def sem(name):
            return t.ctx.enter_context(nc.semaphore(name))

        def two(make, name, *a):
            return [make(f"{name}{u}", *a) for u in range(2)]

        G2 = sb("G2", [P, D])
        yy, xx, oo = two(sb, "yy", [P, 2, D]), two(sb, "xx", [P, D]), two(sb, "oo", [P, D])
        junk = two(sb, "junk2_", [P, D], BF16)
        ss, var, rs = two(sb, "css", [P, 1]), two(sb, "cvar", [P, 1]), two(sb, "crs", [P, 1])
        hp = sb("half_pow2", [P, 2])
        g2_in, hp_set = sem("g2_in"), sem("half_pow_set")
        y_in, x_in, first, moe, ss_done, var_done, rs_done, scaled, added, stored = (two(sem, n) for n in (
            "cy_in", "cx_in", "first_weighted", "moe_ready", "c_ss", "c_var", "c_rstd", "c_scaled", "c_added", "c_stored"))
        yd = dram["y"].rearrange("(n p k) d -> n p k d", p=P, k=2)
        x1d = dram["x1"].rearrange("(n p) d -> n p d", p=P)
        od = dram["out"].rearrange("o (n p) d -> (o n) p d", p=P)
        TURNS = NCH // 2

        block = own.enter_context(nc.Block())

        @block.sync
        def _(sp):
            sp.dma_start(G2[:], dram["g2"].to_broadcast([P, D])).then_inc(g2_in, 16)
            with sp.Fori(0, TURNS) as i:
                for u in range(2):
                    sp.wait_ge(moe[u], i)
                    sp.dma_start(yy[u][:], yd[bass.ds(2 * i + u, 1)].rearrange("o p k d -> (o p) k d")).then_inc(y_in[u], 16)
                    sp.wait_ge(added[u], i)
                    sp.dma_start(xx[u][:], x1d[bass.ds(2 * i + u, 1)].rearrange("o p d -> (o p) d")).then_inc(x_in[u], 16)

        @block.scalar
        def _(act):
            with act.Fori(0, TURNS) as i:
                for u in range(2):
                    act.wait_ge(moe[u], i + 1)
                    act.activation(junk[u][:], oo[u][:], ACT.Square, accum_out=ss[u][:]).then_inc(ss_done[u], 1)
                for u in range(2):
                    act.wait_ge(added[u], i + 1)
                    act.dma_start(od[bass.ds(2 * i + u, 1)].rearrange("o p d -> (o p) d"), oo[u][:]).then_inc(stored[u], 16)
            for u in range(2):
                act.wait_ge(stored[u], 16 * TURNS)

        @block.gpsimd
        def _(pool):
            pool.memset(hp[:, 0:1], -0.5)
            pool.memset(hp[:, 1:2], D * EPS).then_inc(hp_set, 1)
            pool.wait_ge(hp_set, 1)
            with pool.Fori(0, TURNS) as i:
                for u in range(2):
                    pool.wait_ge(ss_done[u], i + 1)
                    pool.tensor_tensor(var[u][:], ss[u][:], hp[:, 1:2], ALU.add).then_inc(var_done[u], 1)
                    pool.wait_ge(var_done[u], i + 1)
                    pool.tensor_tensor(rs[u][:], var[u][:], hp[:, 0:1], ALU.pow).then_inc(rs_done[u], 1)

        @block.vector
        def _(dve):
            dve.wait_ge(g2_in, 16)
            with dve.Fori(0, TURNS) as i:
                for u in range(2):
                    w = r.wts[:, bass.ds(2 * i + u, 1), :].rearrange("p o k -> p (o k)")
                    dve.wait_ge(y_in[u], 16 * (i + 1))
                    dve.wait_ge(stored[u], 16 * i)
                    dve.tensor_scalar(oo[u][:], yy[u][:, 0, :], w[:, 0:1], None, ALU.mult).then_inc(first[u], 1)
                    dve.wait_ge(first[u], i + 1)
                    dve.scalar_tensor_tensor(oo[u][:], yy[u][:, 1, :], w[:, 1:2], oo[u][:], ALU.mult,
                                             ALU.add).then_inc(moe[u], 1)
                for u in range(2):
                    dve.wait_ge(rs_done[u], i + 1)
                    dve.scalar_tensor_tensor(oo[u][:], oo[u][:], rs[u][:], G2[:], ALU.mult, ALU.mult).then_inc(scaled[u], 1)
                    dve.wait_ge(scaled[u], i + 1)
                    dve.wait_ge(x_in[u], 16 * (i + 1))
                    dve.tensor_tensor(oo[u][:], oo[u][:], xx[u][:], ALU.add).then_inc(added[u], 1)


class Tiles:
    pass


def build(nc, dram):
    with ExitStack() as ctx:
        def sb(where, name, shape, dt=F32):
            return where.enter_context(nc.sbuf_tensor(name, shape, dt))

        t, r = Tiles(), Tiles()
        t.ctx = ctx
        t.cst = sb(ctx, "cst", [P, C_MATS, P])
        t.A2, t.B2 = sb(ctx, "A2", [P, KD]), sb(ctx, "B2", [P, KD])
        with ExitStack() as mix:
            t.A1, t.B1 = sb(mix, "A1", [P, KD]), sb(mix, "B1", [P, KD])
            t.chp = sb(mix, "chp", [P, CH_COLS])
            t.G1 = sb(mix, "G1", [P, D])
            t.dnn = sb(mix, "dnn", [P, HD])
            t.gaterow, t.babias = sb(mix, "gaterow", [P, 2 * HEADS]), sb(mix, "babias", [P, 2 * HEADS])
            t.nega, t.halfb = sb(mix, "nega", [P, HEADS]), sb(mix, "halfb", [P, 2 * CFG])
            t.rbias = sb(mix, "rbias", [P, NR])
            t.wr = sb(mix, "wr", [P, KD, NR])
            t.win, t.wout = sb(mix, "win", [P, KD, IN_COLS]), sb(mix, "wout", [P, KD, D])
            build_setup(nc, mix, t, dram)
            build_mixer(nc, t, dram)
        r.ids, r.tok = sb(ctx, "ids", [P, BLOCKS + 2], U32), sb(ctx, "tok", [P, BLOCKS + 2], U32)
        r.info = sb(ctx, "info", [1, 4 * P + 1], I32)
        r.wts = sb(ctx, "wts", [P, NCH, 2])
        build_routing(nc, r, t, dram)
        build_experts(nc, r, t, dram)
        build_combine(nc, r, t, dram)


def _constants():
    p, c = np.arange(P)[:, None], np.arange(P)[None, :]
    mats = [p == c, c >= p, c > p, c < p, np.ones((P, P))]
    mats += [(((p ^ c) >> n) == 1) & (c > p) for n in range(LEVELS)]
    cst = np.stack(mats, axis=1).astype(np.float32)
    io8 = np.broadcast_to(np.stack([np.arange(8), np.arange(8) + 64]), (P, 2, 8)).astype(np.float32)
    iop = np.arange(P, dtype=np.float32)[:, None]
    tok = np.arange(NCH)[None, :] * P + np.arange(P)[:, None]
    ids = np.stack([2 * tok, 2 * tok + 1], axis=2).astype(np.int32)
    return {"cst": cst, "io8": io8, "iop": iop, "ids": ids}


def kernel(**inputs):
    import concourse.bacc as _bacc
    from concourse.bass_utils import run_bass_kernel_spmd as _run

    a = {n: np.asarray(v) for n, v in inputs.items()}

    def cols(v):
        return np.swapaxes(v.reshape((-1, P) + v.shape[1:]), 0, 1)

    def flat(v):
        return np.ascontiguousarray(v).reshape(P, -1)

    chp = np.concatenate([
        flat(cols(a["c"][0])), flat(cols(a["norm_pre_mix"][0])), flat(a["norm_pre_ffn"][0].reshape(P, KD)),
        flat(cols(a["dn_conv_w"][0].T)), flat(cols(a["cf_pw1_b"][0])), flat(cols(a["cf_dw_w"][0].T)),
        flat(cols(a["cf_dw_b"][0])), flat(cols(a["cf_ln_w"][0])), flat(cols(a["cf_ln_b"][0]))], axis=1)
    rows = np.concatenate([a[n][0].reshape(-1) for n in (
        "b_ada", "norm_post_mix", "norm_post_ffn", "dn_norm_w", "dn_a_log", "dn_dt_bias",
        "b_router_group", "b_router_expert")])[None, :]
    w_r = np.concatenate([a["w_router_group"][0], a["w_router_expert"][0]], axis=1).reshape(P, KD, NR)
    feeds = {"x": a["x"][0], "chp": chp, "rows": rows, "w_ada": a["w_ada"][0], "w_in": cols(a["w_in"][0]),
             "w_out": cols(a["w_out"][0]), "w_r": w_r, "w_gate": a["w_gate"][0], "w_up": a["w_up"][0],
             "w_down": a["w_down"][0]}
    feeds.update(_constants())

    nc = _bacc.Bacc("TRN2", target_bir_lowering=False, num_devices=1, dynamic_dma_scratch_size=2048)
    arrays, dram = {}, {}
    for n, v in feeds.items():
        v = np.ascontiguousarray(v)
        arrays[f"in_{n}_dram"] = v
        dram[n] = nc.dram_tensor(f"in_{n}_dram", v.shape, mybir.dt.from_np(v.dtype), kind="ExternalInput").ap()
    for n, shape, dt in (("x1", (SEQ, D), F32), ("h2", (SEQ, D), F32), ("y", (2 * SEQ, D), F32),
                         ("lg", (NCH, P, NR), F32), ("g2", (1, D), F32), ("table", (P * (BLOCKS + 2), 1), U32)):
        dram[n] = nc.dram_tensor(f"{n}_dram", shape, dt, kind=SCRATCH).ap()
    dram["out"] = nc.dram_tensor("out_0_dram", (1, SEQ, D), F32, kind="ExternalOutput").ap()
    build(nc, dram)
    got = _run(nc, [arrays], core_ids=[0])
    return got.results[0]["out_0_dram"]
```

```python
from contextlib import ExitStack

import numpy as np
import concourse.bass as bass
from concourse import mybir
from concourse.alu_op_type import AluOpType as ALU

P = 128
SEQ, D = 2048, 1024
NCH = SEQ // P
KD = D // P
HEADS, HD = 4, 128
DNW = HEADS * HD
CFW = D - DNW
CFG = CFW // P
DNT, CFT = 4, 31
QKVG = 3 * DNW // P
COL_Z, COL_BA, COL_CFA, COL_CFB = 3 * DNW, 4 * DNW, 4 * DNW + 2 * HEADS, 4 * DNW + 2 * HEADS + CFW
IN_COLS = COL_CFB + CFW
LEVELS = 7
NG, EPG = 8, 8
NE = NG * EPG
NR = NG + NE
DE = 512
KE = DE // P
EPS = 1e-6
ROOT_D = float(D) ** 0.5
HB = P // 2
PAIRS = NE // 2
STEPS = 2 * SEQ // HB + PAIRS
SIDE = 1 << 13
FREE_ROW = 1 << 14
SLOTS = 4
SCRATCH = "Internal"

F32, BF16, I32, U32 = mybir.dt.float32, mybir.dt.bfloat16, mybir.dt.int32, mybir.dt.uint32
ACT = mybir.ActivationFunctionType
AXX = mybir.AxisListType.X

CH_C, CH_NPRE, CH_NFFN = 0, KD, 2 * KD
CH_DNW = 3 * KD
CH_CFB = CH_DNW + QKVG * DNT
CH_CFW = CH_CFB + 2 * CFG
CH_DWB = CH_CFW + CFG * CFT
CH_LNW, CH_LNB = CH_DWB + CFG, CH_DWB + 2 * CFG
CH_COLS = CH_DWB + 3 * CFG
C_ID, C_UI, C_US, C_LS, C_ONE, C_LV = 0, 1, 2, 3, 4, 5
C_MATS = 5 + LEVELS
R_ADA, R_NPM, R_NPF = 0, 6 * D, 7 * D
R_DNN = 8 * D
R_ALOG, R_DT, R_RB = R_DNN + HD, R_DNN + HD + HEADS, R_DNN + HD + 2 * HEADS
R_COLS = R_RB + NR


def over_cols(ap, n):
    return ap.unsqueeze(2).to_broadcast([ap.shape[0], ap.shape[1], n])


def over_heads(ap, n):
    return ap.unsqueeze(1).to_broadcast([ap.shape[0], n, ap.shape[1]])


def build_setup(nc, ctx, t, dram):
    with ExitStack() as own:
        def sb(name, shape, dt=F32):
            return own.enter_context(nc.sbuf_tensor(name, shape, dt))

        def sem(name):
            return t.ctx.enter_context(nc.semaphore(name))

        mod = sb("mod", [P, 6 * D])
        wa = [sb(f"wa{s}", [P, KD, 512]) for s in range(2)]
        cact = sb("cact", [P, KD])
        cbc = sb("cbc", [P, KD, P])
        g2 = sb("g2", [P, D])
        cols = sb("modcols", [P, 4, KD])
        pa = [own.enter_context(nc.psum_tensor(f"ada_ps{s}", [P, 512], F32)) for s in range(2)]
        pt = [own.enter_context(nc.psum_tensor(f"modT_ps{s}", [P, KD, P], F32)) for s in range(2)]
        params_in, rows_in, w_in_loaded = sem("params_in"), sem("rows_in"), sem("w_in_loaded")
        wa_in = [sem("wa_in0"), sem("wa_in1")]
        c_silu, c_spread, ada_ps, ada_added = sem("c_silu"), sem("c_spread"), sem("ada_ps"), sem("ada_added")
        modT_ps, modT_read, tail, decay_exp = sem("modT_ps"), sem("modT_read"), sem("setup_tail"), sem("decay_exp")
        g2_out = sem("g2_out")
        NA = 6 * D // 512
        COLS = (0, 1, 3, 4)

        block = own.enter_context(nc.Block())

        @block.sync
        def _(sp):
            sp.dma_start(t.chp[:], dram["chp"]).then_inc(params_in, 16)
            sp.dma_start(t.cst[:], dram["cst"]).then_inc(params_in, 16)
            for n in range(NA):
                if n >= 2:
                    sp.wait_ge(ada_ps, n - 1)
                sp.dma_start(wa[n % 2][:], dram["w_ada"].rearrange("(k p) n -> p k n", p=P)[
                    :, :, n * 512:(n + 1) * 512]).then_inc(wa_in[n % 2], 16)
            sp.wait_ge(tail, 2)
            sp.dma_start(dram["g2"], g2[0:1, :]).then_inc(g2_out, 16)
            sp.wait_ge(g2_out, 16)

        @block.scalar
        def _(act):
            def row(a, n):
                return dram["rows"][:, a:a + n].to_broadcast([P, n])

            act.wait_ge(params_in, 32)
            act.activation(cact[:], t.chp[:, CH_C:CH_C + KD], ACT.Silu).then_inc(c_silu, 1)
            act.dma_start(mod[:], row(R_ADA, 6 * D)).then_inc(rows_in, 16)
            act.dma_start(t.G1[:], row(R_NPM, D)).then_inc(rows_in, 16)
            act.dma_start(g2[:], row(R_NPF, D)).then_inc(rows_in, 16)
            act.dma_start(t.dnn[:], row(R_DNN, HD)).then_inc(rows_in, 16)
            act.dma_start(t.gaterow[:], row(R_ALOG, 2 * HEADS)).then_inc(rows_in, 16)
            act.dma_start(t.rbias[:], row(R_RB, NR)).then_inc(rows_in, 16)
            for k in range(KD):
                act.wait_ge(ada_ps, k + 1)
                act.dma_start(t.win[:, k, :], dram["w_in"][:, k, :]).then_inc(w_in_loaded, 16)
            act.dma_start(t.wout[:], dram["w_out"]).then_inc(w_in_loaded, 16)
            act.dma_start(t.wr[:], dram["w_r"]).then_inc(w_in_loaded, 16)
            act.wait_ge(rows_in, 96)
            act.activation(t.gaterow[:, 0:HEADS], t.gaterow[:, 0:HEADS], ACT.Exp).then_inc(decay_exp, 1)
            act.wait_ge(w_in_loaded, 16 * (KD + 2))

        @block.tensor
        def _(pe):
            pe.wait_ge(c_spread, 1)
            for n in range(NA):
                pe.wait_ge(wa_in[n % 2], 16 * (n // 2 + 1))
                if n >= 2:
                    pe.wait_ge(ada_added, n - 1)
                for k in range(KD):
                    mm = pe.matmul(pa[n % 2][:], cbc[:, k, :], wa[n % 2][:, k, :], start=(k == 0), stop=(k == KD - 1))
                mm.then_inc(ada_ps, 1)
            pe.wait_ge(ada_added, NA)
            for q, m in enumerate(COLS):
                if q >= 2:
                    pe.wait_ge(modT_read, q - 1)
                for k in range(KD):
                    part = mod[:, m * D:(m + 1) * D]
                    part = part[:, k * P:(k + 1) * P] if m < 3 else part.rearrange("p (q k) -> p k q", k=KD)[:, k, :]
                    mm = pe.transpose(pt[q % 2][:, k, :], part, t.cst[:, C_ID, :])
                mm.then_inc(modT_ps, 1)

        @block.vector
        def _(dve):
            dve.wait_ge(c_silu, 1)
            dve.tensor_copy(cbc[:], over_cols(cact[:], P)).then_inc(c_spread, 1)
            dve.wait_ge(rows_in, 96)
            for n in range(NA):
                dve.wait_ge(ada_ps, n + 1)
                m = mod[:, n * 512:(n + 1) * 512]
                dve.tensor_tensor(m, pa[n % 2][:], m, ALU.add).then_inc(ada_added, 1)
            dve.wait_ge(ada_added, NA)
            dve.scalar_tensor_tensor(t.G1[:], t.G1[:], ROOT_D, mod[:, 2 * D:3 * D], ALU.mult, ALU.mult).then_inc(tail, 1)
            dve.scalar_tensor_tensor(g2[:], g2[:], ROOT_D, mod[:, 5 * D:6 * D], ALU.mult, ALU.mult).then_inc(tail, 1)
            for q in range(4):
                dve.wait_ge(modT_ps, q + 1)
                dve.tensor_copy(cols[:, q, :], pt[q % 2][:, :, 0]).then_inc(modT_read, 1)
            dve.wait_ge(modT_read, 4)
            dve.scalar_tensor_tensor(t.A1[:], cols[:, 1, :], 1.0, t.chp[:, CH_NPRE:CH_NPRE + KD], ALU.add, ALU.mult)
            dve.scalar_tensor_tensor(t.A2[:], cols[:, 3, :], 1.0, t.chp[:, CH_NFFN:CH_NFFN + KD], ALU.add, ALU.mult)
            dve.tensor_copy(t.B1[:], cols[:, 0, :])
            dve.tensor_copy(t.B2[:], cols[:, 2, :])
            dve.tensor_scalar(t.halfb[:], t.chp[:, CH_CFB:CH_CFB + 2 * CFG], 0.5, None, ALU.mult)
            dve.wait_ge(decay_exp, 1)
            dve.tensor_scalar(t.nega[:], t.gaterow[:, 0:HEADS], -1.0, None, ALU.mult)
            dve.tensor_scalar(t.dnn[:], t.dnn[:], float(HD) ** 0.5, None, ALU.mult)
            dve.memset(t.babias[:, 0:HEADS], 0.0)
            dve.tensor_copy(t.babias[:, HEADS:2 * HEADS], t.gaterow[:, HEADS:2 * HEADS]).then_inc(tail, 1)
            dve.wait_ge(tail, 3)


def build_mixer(nc, t, dram):
    sems = []
    with ExitStack() as own:
        def sb(name, shape, dt=F32):
            return own.enter_context(nc.sbuf_tensor(name, shape, dt))

        def sem(name):
            sems.append(nc.alloc_semaphore(name))
            return sems[-1]

        xin = sb("xin", [P, D])
        junk = sb("junk", [P, D], BF16)
        hT = sb("hT", [P, KD, P])
        pre = sb("pre", [P, QKVG, DNT - 1 + P])
        cfpre = sb("cfpre", [P, CFG, CFT - 1 + P])
        cv = sb("cv", [P, QKVG, P])
        cvf = sb("cvf", [P, CFG, P])
        glut = sb("glut", [P, CFG, P])
        zn, zg = sb("zn", [P, HEADS, HD]), sb("zg", [P, HEADS, HD])
        small = sb("small", [P, 96])
        qkvT = sb("qkvT", [P, QKVG, P])
        h2n = sb("h2n", [P, D])
        sq = cv[:, 0:2 * HEADS, :]
        x1 = sb("x1", [P, D])
        mixT = sb("mixT", [P, KD, P])
        khat, khatT = sb("khat", [P, HEADS, HD]), sb("khatT", [P, HEADS, P])
        kw, bv = sb("kw", [P, HEADS, HD]), sb("bv", [P, HEADS, HD])
        EU, KT, attnT = sb("EU", [P, HEADS, P]), sb("KT", [P, HEADS, P]), sb("attnT", [P, HEADS, P])
        Kl = [sb("Kl0", [P, HEADS, P]), sb("Kl1", [P, HEADS, P])]
        T, N, Pm, S = (sb(n, [P, HEADS, P]) for n in ("T", "N", "Pm", "S"))
        xc = sb("xc", [P, CFG, P])
        gU, nwT, vn, o1, o2 = Kl[1], Kl[0], Pm, KT, T
        lnsq = sq[:, 0:CFG, :]
        lnd = cv[:, 2 * HEADS, :]
        (ss0, rs0, ss1, rs1, ss2, rs2, v0, v1, v2) = (small[:, n:n + 1] for n in range(9))
        ssn, rqk = small[:, 10:18], small[:, 18:26]
        bal, en, e8 = small[:, 26:34], small[:, 34:42], small[:, 42:50]
        l4, sp4, g4 = small[:, 50:54], small[:, 54:58], small[:, 58:62]
        beta, nbe = small[:, 62:66], small[:, 66:70]
        ex = small[:, 70:82]
        oss, orr = small[:, 82:86], small[:, 86:90]
        eps_d, eps_hd2 = small[:, 90:91], small[:, 91:95]
        hp = sb("half_pow", [P, 8])
        scr = sb("scr", [P, 16])
        lnv, lnr = sb("ln_variance", [P, 1]), sb("ln_rstd", [P, 1])
        lgs = sb("lgs", [P, NR])

        def ps(name, shape):
            return own.enter_context(nc.psum_tensor(name, shape, F32))

        wide = ps("wide_ps", [P, D])
        pj = [ps("pj0_ps", [P, 4, P]), ps("pj1_ps", [P, 4, P])]
        misc = ps("misc_ps", [P, 512])
        b5, b6, b7 = (ps(f"dn{n}_ps", [P, HEADS, P]) for n in range(3))
        wideT = wide[:].rearrange("p (k c) -> p k c", k=KD)
        m_ssq, m_gate, m_ba = misc[:, 0:8], misc[:, 8:20], misc[:, 24:32]
        m_mean, m_lnr, m_lg, m_var = misc[:, 128:256], misc[:, 256:384], misc[:, 384:384 + NR], misc[:, 40:41]

        (x_loaded, x_ss, x_var, x_rstd, xn_ready, xnT_ps, hT_ready) = map(sem, (
            "x_loaded", "x_ss", "x_var", "x_rstd", "xn_ready", "xnT_ps", "hT_ready"))
        (cfa_ps, cfb_ps, q_ps, k_ps, v_ps, z_ps, ba_ps) = map(sem, (
            "cfa_ps", "cfb_ps", "q_ps", "k_ps", "v_ps", "z_ps", "ba_ps"))
        (cfa_evac, cfb_evac, q_evac, k_evac, v_evac, z_evac) = map(sem, (
            "cfa_evac", "cfb_evac", "q_evac", "k_evac", "v_evac", "z_evac"))
        halo_dn, halo_cf, glu_done, cf_tap, dn_tap, z_ready = map(sem, (
            "halo_dn", "halo_cf", "glu_done", "cf_tap", "dn_tap", "z_ready"))
        (ba_biased, ba_neg, ba_exp, ba_ln, beta_den, softplus, g_ready, gU_ready, dec_ps, gates_ps,
         dec_exp, gates_exp, EU_ready, nbe_ready) = map(sem, (
            "ba_biased", "ba_neg", "ba_exp", "ba_ln", "beta_den", "softplus", "g_ready", "gU_ready",
            "dec_ps", "gates_ps", "dec_exp", "gates_exp", "EU_ready", "nbe_ready"))
        (qkv_act, qk_sq, kv_ps, ssq_ps, ssn_ready, rqk_ready, khat_ready, bv_ready, kw_ready, kdec_ready,
         khatT_ps, khatT_ready, kk_ps, attn_ps, KT_ready, attnT_ready) = map(sem, (
            "qkv_act", "qk_sq", "kv_ps", "ssq_ps", "ssn_ready", "rqk_ready", "khat_ready", "bv_ready",
            "kw_ready", "kdec_ready", "khatT_ps", "khatT_ready", "kk_ps", "attn_ps", "KT_ready",
            "attnT_ready"))
        mask_done, p1_ps, p_ready, tp_ps, t_ready, pn_ps, n_ready = map(sem, (
            "mask_done", "p1_ps", "p_ready", "tp_ps", "t_ready", "pn_ps", "n_ready"))
        (wT_ps, nwT_ready, oS_ps, vn_ps, vn_ready, oa_ps, dS_ps, S_decayed, S_ready, o_step, o_ss, o_rs,
         o_gated, oT_ps, oT_ready) = map(sem, (
            "wT_ps", "nwT_ready", "oS_ps", "vn_ps", "vn_ready", "oa_ps", "dS_ps", "S_decayed", "S_ready",
            "o_step", "o_ss", "o_rs", "o_gated", "oT_ps", "oT_ready"))
        (mean_ps, xc_ready, xc_sq, var_ps, lnr_var, lnr_ready, lnd_ready, lnr_ps, cfn_ready, cf_ready) = map(sem, (
            "mean_ps", "xc_ready", "xc_sq", "var_ps", "lnr_var", "lnr_ready", "lnd_ready", "lnr_ps", "cfn_ready",
            "cf_ready"))
        (xr_loaded, mix_ps, mix_ss, mix_var, mix_rstd, mix_normed, x1_ready, x1_ss, x1_var, x1_rstd,
         h2n_ready, x1_out, h2n_out, h2T_ps, h2T_ready, lg_ps, lg_ready, lg_out, pstep, consts_set) = map(sem, (
            "xr_loaded", "mix_ps", "mix_ss", "mix_var", "mix_rstd", "mix_normed", "x1_ready", "x1_ss",
            "x1_var", "x1_rstd", "h2n_ready", "x1_out", "h2n_out", "h2T_ps", "h2T_ready", "lg_ps",
            "lg_ready", "lg_out", "pool_step", "consts_set"))

        ident = t.cst[:, C_ID, :]
        xd = dram["x"].rearrange("(n p) d -> n p d", p=P)
        x1d = dram["x1"].rearrange("(n p) d -> n p d", p=P)
        h2d = dram["h2"].rearrange("(n p) d -> n p d", p=P)

        def chunk(ap, i):
            return ap[bass.ds(i, 1)].rearrange("o p d -> (o p) d")

        ITEMS = ((COL_CFA, 1, cfa_ps, v_evac, 0), (COL_CFB, 0, cfb_ps, z_evac, 0),
                 (0, 1, q_ps, cfa_evac, 1), (DNW, 0, k_ps, cfb_evac, 1), (2 * DNW, 1, v_ps, q_evac, 1))

        block = own.enter_context(nc.Block())

        @block.sync
        def _(sp):
            def load_x(j):
                sp.wait_ge(xnT_ps, j)
                sp.dma_start(xin[:], chunk(xd, j)).then_inc(x_loaded, 16)

            def load_xr(i):
                sp.wait_ge(x1_out, 16 * i)
                sp.wait_ge(x1_rstd, i)
                sp.wait_ge(h2n_ready, i)
                sp.dma_start(x1[:], chunk(xd, i)).then_inc(xr_loaded, 16)

            def stores(i):
                sp.wait_ge(x1_ready, i + 1)
                sp.dma_start(chunk(x1d, i), x1[:]).then_inc(x1_out, 16)
                sp.wait_ge(h2n_ready, i + 1)
                sp.dma_start(chunk(h2d, i), h2n[:]).then_inc(h2n_out, 16)
                sp.wait_ge(lg_ready, i + 1)
                sp.dma_start(chunk(dram["lg"], i), lgs[:]).then_inc(lg_out, 16)

            load_x(0)
            load_x(1)
            with sp.Fori(0, NCH - 2) as i:
                load_x(i + 2)
                load_xr(i)
                stores(i)
            for i in (NCH - 2, NCH - 1):
                load_xr(i)
                stores(i)
            sp.wait_ge(x1_out, 16 * NCH)
            sp.wait_ge(h2n_out, 16 * NCH)
            sp.wait_ge(lg_out, 16 * NCH)

        @block.tensor
        def _(pe):
            def front_transposes(j):
                pe.wait_ge(xn_ready, j + 1)
                pe.wait_ge(v_evac, j)
                pe.wait_ge(z_evac, j)
                for k in range(KD):
                    mm = pe.transpose(pj[1 - k // 4][:, k % 4, :], xin[:, k * P:(k + 1) * P], ident)
                mm.then_inc(xnT_ps, 1)

            def project(j, first, last):
                for g in range(first, last):
                    col, bank, written, reader, same = ITEMS[g // 4]
                    if g == 0:
                        pe.wait_ge(hT_ready, j + 1)
                    if g % 4 == 0:
                        pe.wait_ge(reader, j + same)
                    for k in range(KD):
                        mm = pe.matmul(pj[bank][:, g % 4, :], t.win[:, k, col + (g % 4) * P:col + (g % 4 + 1) * P],
                                       hT[:, k, :], start=(k == 0), stop=(k == KD - 1))
                    if g % 4 == 3:
                        mm.then_inc(written, 1)

            def project_z(j):
                pe.wait_ge(k_evac, j + 1)
                for k in range(KD):
                    mm = pe.matmul(pj[0][:].rearrange("p a b -> p (a b)"), hT[:, k, :], t.win[:, k, COL_Z:COL_Z + DNW],
                                   start=(k == 0), stop=(k == KD - 1))
                mm.then_inc(z_ps, 1)
                pe.wait_ge(cfn_ready, j)
                if not isinstance(j, int) or j > 1:
                    pe.wait_ge(lg_ready, j - 1)
                for k in range(KD):
                    mm = pe.matmul(m_ba, hT[:, k, :], t.win[:, k, COL_BA:COL_BA + 2 * HEADS],
                                   start=(k == 0), stop=(k == KD - 1))
                mm.then_inc(ba_ps, 1)

            def decays(j):
                pe.wait_ge(gU_ready, j + 1)
                pe.wait_ge(oT_ready, j)
                pe.matmul(b7[:], t.cst[:, C_LS, :], gU[:], start=True, stop=True).then_inc(dec_ps, 1)
                pe.matmul(m_gate[:, 0:4], t.cst[:, C_UI, :], g4, start=True, stop=True)
                pe.matmul(m_gate[:, 4:8], t.cst[:, C_LS, :], g4, start=True, stop=True)
                pe.matmul(m_gate[:, 8:12], t.cst[:, C_ONE, :], g4, start=True, stop=True).then_inc(gates_ps, 1)

            def keys(i):
                pe.wait_ge(qkv_act, i + 1)
                pe.wait_ge(S_ready, i)
                pe.wait_ge(o_step, 2 * i)
                for h in range(HEADS):
                    pe.transpose(b5[:, h, :], qkvT[:, HEADS + h, :], ident)
                for h in range(HEADS):
                    mm = pe.transpose(b6[:, h, :], qkvT[:, 2 * HEADS + h, :], ident)
                mm.then_inc(kv_ps, 1)
                pe.wait_ge(qk_sq, i + 1)
                pe.wait_ge(gates_exp, i + 1)
                for h in range(2 * HEADS):
                    mm = pe.matmul(m_ssq[:, h:h + 1], sq[:, h, :], t.cst[:, C_ONE, 0:1], start=True, stop=True)
                mm.then_inc(ssq_ps, 1)

            def ln_mean(i):
                pe.wait_ge(cf_tap, CFT * (i + 1))
                pe.wait_ge(ssn_ready, i + 1)
                for g in range(CFG):
                    mm = pe.matmul(m_mean, t.cst[:, C_ONE, :], cvf[:, g, :], start=(g == 0), stop=(g == CFG - 1))
                mm.then_inc(mean_ps, 1)

            def ln_var(i):
                pe.wait_ge(xc_sq, i + 1)
                for g in range(CFG):
                    mm = pe.matmul(m_var, lnsq[:, g, :], t.cst[:, C_ONE, 0:1], start=(g == 0), stop=(g == CFG - 1))
                mm.then_inc(var_ps, 1)

            def ln_spread(i):
                pe.wait_ge(lnd_ready, i + 1)
                pe.matmul(m_lnr, t.cst[:, C_ONE, :], lnd, start=True, stop=True).then_inc(lnr_ps, 1)

            def scores(i):
                pe.wait_ge(khatT_ready, i + 1)
                pe.wait_ge(bv_ready, i + 1)
                for h in range(HEADS):
                    mm = pe.matmul(b6[:, h, :], khatT[:, h, :], khatT[:, h, :], start=True, stop=True)
                mm.then_inc(kk_ps, 1)
                pe.wait_ge(dec_exp, i + 1)
                for h in range(HEADS):
                    mm = pe.matmul(b7[:, h, :], khatT[:, h, :], qkvT[:, h, :], start=True, stop=True)
                mm.then_inc(attn_ps, 1)

            def level_p(i, l):
                pe.wait_ge(mask_done, i * LEVELS + l + 1)
                if l > 0:
                    pe.wait_ge(t_ready, i * (LEVELS - 1) + l)
                else:
                    pe.wait_ge(khatT_ready, i + 1)
                for h in range(HEADS):
                    mm = pe.matmul(b5[:, h, :], Kl[l % 2][:, h, :], ident if l == 0 else T[:, h, :], start=True, stop=True)
                mm.then_inc(p1_ps, 1)

            def level_tn(i, l):
                pe.wait_ge(p_ready, i * LEVELS + l + 1)
                if l == 0:
                    pe.wait_ge(attnT_ready, i + 1)
                else:
                    pe.wait_ge(n_ready, i * LEVELS + l)
                if l < LEVELS - 1:
                    for h in range(HEADS):
                        mm = pe.matmul(b6[:, h, :], ident if l == 0 else N[:, h, :], Pm[:, h, :], start=True, stop=True)
                    mm.then_inc(tp_ps, 1)
                for h in range(HEADS):
                    mm = pe.matmul(b7[:, h, :], Pm[:, h, :], ident if l == 0 else N[:, h, :], start=True, stop=True)
                mm.then_inc(pn_ps, 1)

            def scan(i, j):
                pe.wait_ge(n_ready, LEVELS * (i + 1))
                pe.wait_ge(kw_ready, i + 1)
                for h in range(HEADS):
                    mm = pe.matmul(b5[:, h, :], kw[:, h, :], N[:, h, :], start=True, stop=True)
                mm.then_inc(wT_ps, 1)
                for h in range(HEADS):
                    mm = pe.matmul(b7[:, h, :], qkvT[:, h, :], S[:, h, :], start=True, stop=True)
                mm.then_inc(oS_ps, 1)
                pe.wait_ge(nwT_ready, i + 1)
                for h in range(HEADS):
                    pe.matmul(b6[:, h, :], N[:, h, :], bv[:, h, :], start=True, stop=False)
                    mm = pe.matmul(b6[:, h, :], nwT[:, h, :], S[:, h, :], start=False, stop=True)
                mm.then_inc(vn_ps, 1)
                pe.wait_ge(vn_ready, i + 1)
                pe.wait_ge(kdec_ready, i + 1)
                for h in range(HEADS):
                    mm = pe.matmul(b6[:, h, :], khat[:, h, :], vn[:, h, :], start=True, stop=True)
                mm.then_inc(dS_ps, 1)
                for h in range(HEADS):
                    mm = pe.matmul(b5[:, h, :], attnT[:, h, :], vn[:, h, :], start=True, stop=True)
                mm.then_inc(oa_ps, 1)

            def head_transposes(i):
                pe.wait_ge(o_gated, i + 1)
                for h in range(HEADS):
                    mm = pe.transpose(b7[:, h, :], o1[:, h, :], ident)
                mm.then_inc(oT_ps, 1)

            def project_out(i, first, last):
                if first:
                    pe.wait_ge(cf_ready, i + 1)
                    pe.wait_ge(h2T_ready, i)
                else:
                    pe.wait_ge(oT_ready, i + 1)
                for half in range(2):
                    for k in range(first, last):
                        mm = pe.matmul(wide[:, half * 512:(half + 1) * 512], mixT[:, k, :],
                                       t.wout[:, k, half * 512:(half + 1) * 512], start=(k == HEADS), stop=(k == HEADS - 1))
                if not first:
                    mm.then_inc(mix_ps, 1)

            def router_transposes(i):
                pe.wait_ge(h2n_ready, i + 1)
                hv = h2n[:].rearrange("p (q k) -> p k q", k=KD)
                for k in range(KD):
                    mm = pe.transpose(wideT[:, k, :], hv[:, k, :], ident)
                mm.then_inc(h2T_ps, 1)

            def router(i, lns):
                pe.wait_ge(h2T_ready, i + 1)
                pe.wait_ge(cfn_ready, lns)
                for k in range(KD):
                    mm = pe.matmul(m_lg, mixT[:, k, :], t.wr[:, k, :], start=(k == 0), stop=(k == KD - 1))
                mm.then_inc(lg_ps, 1)

            def turn(i, before, front, ahead):
                j = i + 1
                keys(i)
                if front:
                    project(j, 0, 4)
                pe.wait_ge(khat_ready, i + 1)
                for h in range(HEADS):
                    mm = pe.transpose(b5[:, h, :], khat[:, h, :], ident)
                mm.then_inc(khatT_ps, 1)
                if front:
                    project(j, 4, 5)
                scores(i)
                if before:
                    router_transposes(i - 1)
                if front:
                    project(j, 5, 7)
                ln_mean(i)
                for l in range(LEVELS):
                    level_p(i, l)
                    if front:
                        project(j, 7 + (13 * 2 * l) // 14, 7 + (13 * (2 * l + 1)) // 14)
                    level_tn(i, l)
                    if front:
                        project(j, 7 + (13 * (2 * l + 1)) // 14, 7 + (13 * (2 * l + 2)) // 14)
                    if l == 0:
                        ln_var(i)
                    if l == 1:
                        ln_spread(i)
                    if before and l == 2:
                        router(i - 1, i + 1)
                scan(i, j)
                if front:
                    project_z(j)
                if ahead:
                    front_transposes(i + 2)
                project_out(i, HEADS, KD)
                head_transposes(i)
                project_out(i, 0, HEADS)
                if front:
                    decays(j)

            pe.wait_ge(consts_set, 1)
            front_transposes(0)
            project(0, 0, 20)
            project_z(0)
            front_transposes(1)
            decays(0)
            turn(0, False, True, True)
            with pe.Fori(1, NCH - 2) as i:
                turn(i, True, True, True)
            turn(NCH - 2, True, True, False)
            turn(NCH - 1, True, False, False)
            router_transposes(NCH - 1)
            router(NCH - 1, NCH)

        @block.scalar
        def _(act):
            def front_ss(j):
                act.wait_ge(x_loaded, 16 * (j + 1))
                act.wait_ge(x_rstd, j)
                act.activation(junk[:], xin[:], ACT.Square, accum_out=ss0).then_inc(x_ss, 1)

            def front_hT(j):
                act.wait_ge(xnT_ps, j + 1)
                act.wait_ge(ba_ps, j)
                for k in range(KD):
                    ins = act.activation(hT[:, k, :], pj[1 - k // 4][:, k % 4, :], ACT.Identity, bias=t.B1[:, k:k + 1],
                                         scale=t.A1[:, k:k + 1])
                ins.then_inc(hT_ready, 1)

            def front_glu_a(j):
                act.wait_ge(cfa_ps, j + 1)
                act.wait_ge(halo_cf, j + 1)
                for g in range(CFG):
                    ins = act.activation(cfpre[:, g, CFT - 1:], pj[1][:, g, :], ACT.Identity, bias=t.halfb[:, g:g + 1], scale=0.5)
                ins.then_inc(cfa_evac, 1)

            def front_glu_b(j):
                act.wait_ge(cfb_ps, j + 1)
                act.wait_ge(glu_done, j)
                for g in range(CFG):
                    ins = act.activation(glut[:, g, :], pj[0][:, g, :], ACT.Tanh,
                                         bias=t.halfb[:, CFG + g:CFG + g + 1], scale=0.5)
                ins.then_inc(cfb_evac, 1)

            def front_qkv(j, n, written, evac):
                act.wait_ge(written, j + 1)
                if n == 0:
                    act.wait_ge(halo_dn, j + 1)
                bank = pj[1 - n % 2]
                act.copy(pre[:, 4 * n:4 * n + 4, DNT - 1:], bank[:]).then_inc(evac, 1)

            def front_z(j):
                act.wait_ge(z_ps, j + 1)
                act.wait_ge(z_ready, j)
                act.activation(zn[:], pj[0][:], ACT.Silu).then_inc(z_evac, 1)

            def front_gates(j):
                act.wait_ge(ba_neg, j + 1)
                act.wait_ge(beta_den, j)
                act.activation(e8, en, ACT.Exp).then_inc(ba_exp, 1)
                act.wait_ge(ba_exp, j + 1)
                act.activation(l4, e8[:, 4:8], ACT.Ln, bias=1.0).then_inc(ba_ln, 1)

            def front_decays(j):
                act.wait_ge(dec_ps, j + 1)
                act.wait_ge(attnT_ready, j)
                act.activation(EU[:], b7[:], ACT.Exp).then_inc(dec_exp, 1)
                act.wait_ge(gates_ps, j + 1)
                act.wait_ge(S_decayed, j)
                act.wait_ge(o_step, 2 * j)
                act.activation(ex, m_gate, ACT.Exp).then_inc(gates_exp, 1)

            def qkv(i):
                act.wait_ge(dn_tap, 12 * (i + 1))
                act.wait_ge(oS_ps, i)
                act.activation(qkvT[:], cv[:], ACT.Silu).then_inc(qkv_act, 1)
                act.wait_ge(qkv_act, i + 1)
                act.activation(sq[:], qkvT[:, 0:2 * HEADS, :], ACT.Square).then_inc(qk_sq, 1)

            def khat_evac(i):
                act.wait_ge(khatT_ps, i + 1)
                act.copy(khatT[:], b5[:]).then_inc(khatT_ready, 1)

            def ln_square(i):
                act.wait_ge(xc_ready, i + 1)
                act.wait_ge(ssq_ps, i + 1)
                act.activation(lnsq, xc[:], ACT.Square).then_inc(xc_sq, 1)

            def ln_act(i):
                act.wait_ge(cfn_ready, i + 1)
                act.wait_ge(lg_ps, i)
                for g in range(CFG):
                    ins = act.activation(mixT[:, HEADS + g, :], xc[:, g, :], ACT.Silu,
                                         bias=t.chp[:, CH_LNB + g:CH_LNB + g + 1],
                                         scale=t.chp[:, CH_LNW + g:CH_LNW + g + 1])
                ins.then_inc(cf_ready, 1)

            def scan(i):
                act.wait_ge(wT_ps, i + 1)
                act.copy(nwT[:], b5[:]).then_inc(nwT_ready, 1)
                act.wait_ge(vn_ps, i + 1)
                act.copy(vn[:], b6[:]).then_inc(vn_ready, 1)

            def heads(i):
                act.wait_ge(oT_ps, i + 1)
                act.copy(mixT[:, 0:HEADS, :], b7[:]).then_inc(oT_ready, 1)

            def mix_squares(i):
                act.wait_ge(mix_ps, i + 1)
                act.activation(junk[:], wide[:], ACT.Square, accum_out=ss1).then_inc(mix_ss, 1)

            def x1_squares(i):
                act.wait_ge(x1_ready, i + 1)
                act.activation(junk[:], x1[:], ACT.Square, accum_out=ss2).then_inc(x1_ss, 1)

            def h2(i):
                act.wait_ge(h2T_ps, i + 1)
                for k in range(KD):
                    ins = act.activation(mixT[:, k, :], wideT[:, k, :], ACT.Identity, bias=t.B2[:, k:k + 1],
                                         scale=t.A2[:, k:k + 1])
                ins.then_inc(h2T_ready, 1)

            def turn(i, before, front, ahead):
                j = i + 1
                if before:
                    mix_squares(i - 1)
                    x1_squares(i - 1)
                khat_evac(i)
                if front:
                    front_glu_a(j)
                if before:
                    h2(i - 1)
                ln_square(i)
                if front:
                    front_glu_b(j)
                    front_qkv(j, 0, q_ps, q_evac)
                ln_act(i)
                if ahead:
                    front_ss(i + 2)
                if front:
                    front_qkv(j, 1, k_ps, k_evac)
                    front_qkv(j, 2, v_ps, v_evac)
                scan(i)
                if front:
                    front_z(j)
                if ahead:
                    front_hT(i + 2)
                if front:
                    front_gates(j)
                heads(i)
                if front:
                    qkv(j)
                    front_decays(j)

            front_ss(0)
            front_hT(0)
            front_glu_a(0)
            front_glu_b(0)
            front_qkv(0, 0, q_ps, q_evac)
            front_qkv(0, 1, k_ps, k_evac)
            front_qkv(0, 2, v_ps, v_evac)
            front_z(0)
            front_ss(1)
            front_hT(1)
            front_gates(0)
            front_decays(0)
            qkv(0)
            turn(0, False, True, True)
            with act.Fori(1, NCH - 2) as i:
                turn(i, True, True, True)
            turn(NCH - 2, True, True, False)
            turn(NCH - 1, True, False, False)
            mix_squares(NCH - 1)
            x1_squares(NCH - 1)
            h2(NCH - 1)

        @block.gpsimd
        def _(pool):
            def rsqrt_row(src, mid, dst, after, var, done, j):
                pool.wait_ge(after, j + 1)
                pool.tensor_tensor(mid, src, eps_d, ALU.add).then_inc(var, 1)
                pool.wait_ge(var, j + 1)
                pool.tensor_tensor(dst, mid, hp[:, 0:1], ALU.pow).then_inc(done, 1)

            def front_rstd(j):
                pool.wait_ge(xn_ready, j)
                rsqrt_row(ss0, v0, rs0, x_ss, x_var, x_rstd, j)

            def front_z(j):
                pool.wait_ge(z_evac, j + 1)
                pool.wait_ge(o_gated, j)
                pool.tensor_tensor(zg[:], zn[:], over_heads(t.dnn[:], HEADS), ALU.mult).then_inc(z_ready, 1)

            def front_gU(j):
                pool.wait_ge(g_ready, j + 1)
                pool.wait_ge(p1_ps, LEVELS * j)
                pool.tensor_tensor(gU[:], over_heads(t.cst[:, C_UI, :], HEADS), over_cols(g4, P),
                                   ALU.mult).then_inc(gU_ready, 1)

            def front_EU(j):
                pool.wait_ge(dec_exp, j + 1)
                pool.tensor_tensor(EU[:], EU[:], over_heads(t.cst[:, C_UI, :], HEADS), ALU.mult).then_inc(EU_ready, 1)

            def keys(i):
                pool.wait_ge(ssn_ready, i + 1)
                pool.wait_ge(o_rs, i)
                pool.tensor_tensor(rqk, ssn, hp[:, 0:8], ALU.pow).then_inc(rqk_ready, 1)
                pool.wait_ge(khat_ready, i + 1)
                pool.wait_ge(nbe_ready, i + 1)
                pool.tensor_tensor(kw[:], khat[:], over_cols(nbe, P), ALU.mult).then_inc(kw_ready, 1)

            def key_decay(i):
                pool.wait_ge(khatT_ps, i + 1)
                pool.wait_ge(kw_ready, i + 1)
                pool.tensor_tensor(khat[:], khat[:], over_cols(ex[:, 4:8], P), ALU.mult).then_inc(kdec_ready, 1)

            def mask(i, l):
                if l == 0:
                    pool.wait_ge(KT_ready, i + 1)
                    pool.wait_ge(vn_ps, i)
                else:
                    pool.wait_ge(p1_ps, i * LEVELS + max(l - 1, 0))
                pool.tensor_tensor(Kl[l % 2][:], KT[:], over_heads(t.cst[:, C_LV + l, :], HEADS),
                                   ALU.mult).then_inc(mask_done, 1)

            def ln_rstd(i):
                pool.wait_ge(lnr_var, i + 1)
                pool.tensor_tensor(lnr[:], lnv[:], hp[:, 0:1], ALU.pow).then_inc(lnr_ready, 1)
                pool.wait_ge(lnr_ready, i + 1)
                pool.wait_ge(lnr_ps, i)
                pool.tensor_tensor(lnd, ident, lnr[:].to_broadcast([P, P]), ALU.mult).then_inc(lnd_ready, 1)

            def state(i):
                pool.wait_ge(vn_ps, i + 1)
                pool.wait_ge(oS_ps, i + 1)
                pool.tensor_tensor(S[:], S[:], over_cols(ex[:, 8:12], P), ALU.mult).then_inc(S_decayed, 1)

            def head_rstd(i):
                pool.wait_ge(o_ss, i + 1)
                step = 4 * i
                pool.tensor_tensor(scr[:, 0:4], rqk[:, 0:4], rqk[:, 0:4], ALU.mult).then_inc(pstep, 1)
                pool.wait_ge(pstep, step + 1)
                pool.tensor_tensor(scr[:, 4:8], scr[:, 0:4], oss, ALU.mult).then_inc(pstep, 1)
                pool.wait_ge(pstep, step + 2)
                pool.tensor_tensor(scr[:, 8:12], scr[:, 4:8], eps_hd2, ALU.add).then_inc(pstep, 1)
                pool.wait_ge(pstep, step + 3)
                pool.tensor_tensor(scr[:, 12:16], scr[:, 8:12], hp[:, 0:4], ALU.pow).then_inc(pstep, 1)
                pool.wait_ge(pstep, step + 4)
                pool.tensor_tensor(orr, scr[:, 12:16], rqk[:, 0:4], ALU.mult).then_inc(o_rs, 1)

            pool.memset(hp[:], -0.5)
            pool.memset(eps_d, D * EPS)
            pool.memset(eps_hd2, HD * HD * EPS)
            pool.memset(S[:], 0.0)
            pool.memset(pre[:, :, 0:DNT - 1], 0.0)
            pool.memset(cfpre[:, :, 0:CFT - 1], 0.0).then_inc(consts_set, 1)
            pool.wait_ge(consts_set, 1)
            def turn(i, before, front, ahead):
                j = i + 1
                if before:
                    rsqrt_row(ss1, v1, rs1, mix_ss, mix_var, mix_rstd, i - 1)
                keys(i)
                if before:
                    rsqrt_row(ss2, v2, rs2, x1_ss, x1_var, x1_rstd, i - 1)
                key_decay(i)
                mask(i, 0)
                mask(i, 1)
                mask(i, 2)
                ln_rstd(i)
                for l in range(3, LEVELS):
                    mask(i, l)
                if ahead:
                    front_rstd(i + 2)
                state(i)
                head_rstd(i)
                if front:
                    front_z(j)
                    front_gU(j)
                    front_EU(j)

            front_rstd(0)
            front_z(0)
            front_rstd(1)
            front_gU(0)
            front_EU(0)
            turn(0, False, True, True)
            with pool.Fori(1, NCH - 2) as i:
                turn(i, True, True, True)
            turn(NCH - 2, True, True, False)
            turn(NCH - 1, True, False, False)
            rsqrt_row(ss1, v1, rs1, mix_ss, mix_var, mix_rstd, NCH - 1)
            rsqrt_row(ss2, v2, rs2, x1_ss, x1_var, x1_rstd, NCH - 1)

        @block.vector
        def _(dve):
            def front_xn(j):
                dve.wait_ge(x_rstd, j + 1)
                dve.wait_ge(x_ss, j + 1)
                dve.tensor_scalar(xin[:], xin[:], rs0, ROOT_D, ALU.mult, ALU.mult).then_inc(xn_ready, 1)

            def halo_q(j):
                dve.wait_ge(v_evac, j)
                dve.wait_ge(dn_tap, 12 * j)
                dve.tensor_copy(pre[:, :, 0:DNT - 1], pre[:, :, P:P + DNT - 1]).then_inc(halo_dn, 1)

            def halo_c(j):
                dve.wait_ge(cf_tap, CFT * j)
                dve.tensor_copy(cfpre[:, :, 0:CFT - 1], cfpre[:, :, P:P + CFT - 1]).then_inc(halo_cf, 1)

            def front_glu(j):
                dve.wait_ge(cfa_evac, j + 1)
                dve.wait_ge(cfb_evac, j + 1)
                dve.wait_ge(halo_cf, j + 1)
                new = cfpre[:, :, CFT - 1:]
                dve.scalar_tensor_tensor(new, glut[:], 1.0, new, ALU.add, ALU.mult).then_inc(glu_done, 1)

            def cf_rounds(j, first, last):
                for r in range(first, last):
                    if r == 0:
                        dve.wait_ge(glu_done, j + 1)
                        dve.wait_ge(mean_ps, j)
                        dve.wait_ge(xc_ready, j)
                    else:
                        dve.wait_ge(cf_tap, j * CFT + r)
                    for g in range(CFG):
                        w = t.chp[:, CH_CFW + g * CFT + r:CH_CFW + g * CFT + r + 1]
                        src = cfpre[:, g, r:r + P]
                        if r == 0:
                            ins = dve.tensor_scalar(cvf[:, g, :], src, w, t.chp[:, CH_DWB + g:CH_DWB + g + 1],
                                                    ALU.mult, ALU.add)
                        else:
                            ins = dve.scalar_tensor_tensor(cvf[:, g, :], src, w, cvf[:, g, :], ALU.mult, ALU.add)
                    ins.then_inc(cf_tap, 1)

            def dn_conv(j, n, evac):
                dve.wait_ge(evac, j + 1)
                if n == 0:
                    dve.wait_ge(qkv_act, j)
                    dve.wait_ge(ssq_ps, j)
                    dve.wait_ge(lnr_ps, j)
                    dve.wait_ge(halo_dn, j + 1)
                for r in range(DNT):
                    if r > 0:
                        dve.wait_ge(dn_tap, j * 12 + n * DNT + r)
                    for g in range(4 * n, 4 * n + 4):
                        w = t.chp[:, CH_DNW + g * DNT + r:CH_DNW + g * DNT + r + 1]
                        src = pre[:, g, r:r + P]
                        if r == 0:
                            ins = dve.tensor_scalar(cv[:, g, :], src, w, None, ALU.mult)
                        else:
                            ins = dve.scalar_tensor_tensor(cv[:, g, :], src, w, cv[:, g, :], ALU.mult, ALU.add)
                    ins.then_inc(dn_tap, 1)

            def front_ba(j):
                dve.wait_ge(ba_ps, j + 1)
                dve.wait_ge(ba_exp, j)
                dve.tensor_tensor(bal, m_ba, t.babias[:], ALU.add).then_inc(ba_biased, 1)
                dve.wait_ge(ba_biased, j + 1)
                dve.tensor_scalar(en[:, 0:4], bal[:, 0:4], -1.0, None, ALU.mult)
                dve.scalar_tensor_tensor(en[:, 4:8], bal[:, 4:8], -1.0, bal[:, 4:8], ALU.mult, ALU.min).then_inc(ba_neg, 1)

            def front_g(j):
                dve.wait_ge(ba_exp, j + 1)
                dve.tensor_scalar(beta, e8[:, 0:4], 1.0, None, ALU.add).then_inc(beta_den, 1)
                dve.wait_ge(ba_ln, j + 1)
                dve.scalar_tensor_tensor(sp4, bal[:, 4:8], 0.0, l4, ALU.max, ALU.add).then_inc(softplus, 1)
                dve.wait_ge(beta_den, j + 1)
                dve.reciprocal(beta, beta)
                dve.wait_ge(softplus, j + 1)
                dve.wait_ge(gates_ps, j)
                dve.tensor_tensor(g4, sp4, t.nega[:], ALU.mult).then_inc(g_ready, 1)

            def front_nbe(j):
                dve.wait_ge(gates_exp, j + 1)
                dve.wait_ge(g_ready, j + 1)
                dve.scalar_tensor_tensor(nbe, beta, -1.0, ex[:, 0:4], ALU.mult, ALU.mult).then_inc(nbe_ready, 1)

            def keys(i):
                dve.wait_ge(ssq_ps, i + 1)
                dve.tensor_scalar(ssn, m_ssq, EPS, None, ALU.add).then_inc(ssn_ready, 1)

            def khats(i):
                dve.wait_ge(kv_ps, i + 1)
                dve.wait_ge(g_ready, i + 1)
                dve.tensor_tensor(bv[:], b6[:], over_cols(beta, P), ALU.mult).then_inc(bv_ready, 1)
                dve.wait_ge(rqk_ready, i + 1)
                dve.wait_ge(dS_ps, i)
                dve.tensor_tensor(khat[:], b5[:], over_cols(rqk[:, 4:8], P), ALU.mult).then_inc(khat_ready, 1)

            def ln_center(i):
                dve.wait_ge(mean_ps, i + 1)
                dve.wait_ge(cf_ready, i)
                dve.scalar_tensor_tensor(xc[:], over_heads(m_mean, CFG), -1.0 / CFW, cvf[:], ALU.mult,
                                         ALU.add).then_inc(xc_ready, 1)

            def ln_eps(i):
                dve.wait_ge(var_ps, i + 1)
                dve.wait_ge(lnr_ready, i)
                dve.tensor_scalar(lnv[:], m_var, 1.0 / CFW, EPS, ALU.mult, ALU.add).then_inc(lnr_var, 1)

            def ln_scale(i):
                dve.wait_ge(lnr_ps, i + 1)
                dve.wait_ge(xc_sq, i + 1)
                dve.tensor_tensor(xc[:], xc[:], over_heads(m_lnr, CFG), ALU.mult).then_inc(cfn_ready, 1)

            def scores(i):
                dve.wait_ge(kk_ps, i + 1)
                dve.wait_ge(EU_ready, i + 1)
                dve.wait_ge(oT_ps, i)
                dve.tensor_tensor(KT[:], b6[:], EU[:], ALU.mult).then_inc(KT_ready, 1)
                dve.wait_ge(attn_ps, i + 1)
                dve.wait_ge(oa_ps, i)
                dve.tensor_tensor(attnT[:], b7[:], EU[:], ALU.mult).then_inc(attnT_ready, 1)

            def level_p(i, l):
                dve.wait_ge(p1_ps, i * LEVELS + l + 1)
                if l == 0:
                    dve.wait_ge(dS_ps, i)
                    dve.wait_ge(oa_ps, i)
                else:
                    dve.wait_ge(pn_ps, i * LEVELS + l)
                dve.tensor_tensor(Pm[:], b5[:], over_cols(beta, P), ALU.mult).then_inc(p_ready, 1)

            def level_t(i, l):
                if l < LEVELS - 1:
                    dve.wait_ge(tp_ps, i * (LEVELS - 1) + l + 1)
                    if l == 0:
                        dve.wait_ge(o_ss, i)
                    else:
                        dve.wait_ge(t_ready, i * (LEVELS - 1) + l)
                    dve.tensor_tensor(T[:], over_heads(ident, HEADS) if l == 0 else T[:], b6[:],
                                      ALU.subtract).then_inc(t_ready, 1)

            def level_n(i, l):
                dve.wait_ge(pn_ps, i * LEVELS + l + 1)
                if l == 0:
                    dve.wait_ge(vn_ps, i)
                else:
                    dve.wait_ge(n_ready, i * LEVELS + l)
                dve.tensor_tensor(N[:], over_heads(ident, HEADS) if l == 0 else N[:], b7[:],
                                  ALU.subtract).then_inc(n_ready, 1)

            def output(i):
                dve.wait_ge(oS_ps, i + 1)
                dve.wait_ge(mask_done, (i + 1) * LEVELS)
                dve.wait_ge(gates_exp, i + 1)
                dve.tensor_tensor(o1[:], b7[:], over_cols(ex[:, 0:4], P), ALU.mult).then_inc(o_step, 1)
                dve.wait_ge(dS_ps, i + 1)
                dve.wait_ge(S_decayed, i + 1)
                dve.tensor_tensor(S[:], S[:], b6[:], ALU.add).then_inc(S_ready, 1)
                dve.wait_ge(oa_ps, i + 1)
                dve.wait_ge(o_step, 2 * i + 1)
                dve.tensor_tensor(o1[:], o1[:], b5[:], ALU.add).then_inc(o_step, 1)
                dve.wait_ge(o_step, 2 * i + 2)
                dve.wait_ge(p1_ps, (i + 1) * LEVELS)
                dve.tensor_tensor(o2[:], o1[:], o1[:], ALU.mult).then_inc(o2_ready, 1)
                dve.wait_ge(o2_ready, i + 1)
                dve.tensor_reduce(oss, o2[:], AXX, ALU.add).then_inc(o_ss, 1)

            def gate(i):
                dve.wait_ge(o_rs, i + 1)
                dve.tensor_tensor(o1[:], o1[:], over_cols(orr, P), ALU.mult).then_inc(o_scaled, 1)
                dve.wait_ge(z_ready, i + 1)
                dve.wait_ge(o_scaled, i + 1)
                dve.tensor_tensor(o1[:], o1[:], zg[:], ALU.mult).then_inc(o_gated, 1)

            def post(i):
                dve.wait_ge(mix_rstd, i + 1)
                dve.wait_ge(h2n_out, 16 * i)
                dve.wait_ge(h2T_ps, i)
                dve.scalar_tensor_tensor(h2n[:], wide[:], rs1, t.G1[:], ALU.mult, ALU.mult).then_inc(mix_normed, 1)
                dve.wait_ge(mix_normed, i + 1)
                dve.wait_ge(xr_loaded, 16 * (i + 1))
                dve.tensor_tensor(x1[:], x1[:], h2n[:], ALU.add).then_inc(x1_ready, 1)

            def h2(i):
                dve.wait_ge(x1_rstd, i + 1)
                dve.wait_ge(x1_ready, i + 1)
                dve.tensor_scalar(h2n[:], x1[:], rs2, ROOT_D, ALU.mult, ALU.mult).then_inc(h2n_ready, 1)

            def logits(i):
                dve.wait_ge(lg_ps, i + 1)
                dve.wait_ge(lg_out, 16 * i)
                dve.tensor_tensor(lgs[:], m_lg, t.rbias[:], ALU.add).then_inc(lg_ready, 1)

            o2_ready, o_scaled = sem("o2_ready"), sem("o_scaled")

            def turn(i, before, front, ahead):
                j = i + 1
                keys(i)
                if front:
                    halo_q(j)
                if before:
                    post(i - 1)
                khats(i)
                cf_rounds(i, LATE, CFT)
                if front:
                    halo_c(j)
                if before:
                    h2(i - 1)
                scores(i)
                ln_center(i)
                for l in range(LEVELS):
                    r = 3 * (l - 1)
                    level_p(i, l)
                    if front and l > 0:
                        cf_rounds(j, r, r + 2)
                    level_t(i, l)
                    level_n(i, l)
                    if l == 0:
                        ln_eps(i)
                        if front:
                            front_glu(j)
                    if l == 2:
                        ln_scale(i)
                    if l == 3 and before:
                        logits(i - 1)
                    if front and 0 < l < LEVELS - 1:
                        cf_rounds(j, r + 2, r + 3)
                if ahead:
                    front_xn(i + 2)
                if front:
                    dn_conv(j, 0, q_evac)
                    dn_conv(j, 1, k_evac)
                output(i)
                if front:
                    dn_conv(j, 2, v_evac)
                gate(i)
                if front:
                    front_ba(j)
                    cf_rounds(j, 17, 21)
                    front_g(j)
                    cf_rounds(j, 21, LATE)
                    front_nbe(j)

            LATE = 27
            front_xn(0)
            dve.wait_ge(consts_set, 1)
            dve.engine_nop().then_inc(halo_dn, 1)
            dve.engine_nop().then_inc(halo_cf, 1)
            front_glu(0)
            cf_rounds(0, 0, LATE)
            dn_conv(0, 0, q_evac)
            front_xn(1)
            front_ba(0)
            dn_conv(0, 1, k_evac)
            front_g(0)
            dn_conv(0, 2, v_evac)
            front_nbe(0)
            turn(0, False, True, True)
            with dve.Fori(1, NCH - 2) as i:
                turn(i, True, True, True)
            turn(NCH - 2, True, True, False)
            turn(NCH - 1, True, False, False)
            post(NCH - 1)
            h2(NCH - 1)
            logits(NCH - 1)
    nc.clear_and_free_semaphores(sems)
    nc.all_engine_barrier()


def load_gate_up(sp, r, dram, experts, u, landed):
    for m, (w, done) in enumerate((("w_gate", r.gate_in), ("w_up", r.up_in))):
        for side in range(2):
            if m:
                sp.wait_ge(r.gate_in[u][side], landed)
            sp.dma_start(r.wgu[:, 2 * u + side, m * KD:(m + 1) * KD, :].rearrange("p k f -> p (k f)"),
                         dram[w][bass.ds(experts[side], 1)].rearrange("o (p k) f -> p (o k f)", p=P)).then_inc(
                             done[u][side], 16)


def experts_of(sp, r, i, u):
    return [sp.value_load(r.info[0:1, bass.ds(4 * i + 2 * u + side, 1)], min_val=0, max_val=NE - 1) for side in range(2)]


def build_routing(nc, r, t, dram):
    with ExitStack() as own:
        def sb(name, shape, dt=F32):
            return own.enter_context(nc.sbuf_tensor(name, shape, dt))

        def sem(name):
            return t.ctx.enter_context(nc.semaphore(name))

        lg = sb("lg_all", [P, NCH, NR])
        ids0 = sb("ids0", [P, NCH, 2], I32)
        io8 = sb("io8", [P, 2, NG])
        iop = sb("iop", [P, 1])
        gm, gs, m1, m2, ix, ew, dk = (sb(n, [P, NCH]) for n in ("gm", "gs", "m1", "m2", "ix", "ew", "dk"))
        ge, eq, ohg, sel, oh1, oh2, sel2 = (sb(n, [P, NCH, NG]) for n in ("ge", "eq", "ohg", "sel", "oh1", "oh2", "sel2"))
        M1, M2, MM, CC, V = (sb(n, [P, NCH, NG, EPG]) for n in ("M1", "M2", "MM", "CC", "V"))
        tot, keyrow, cmp_, perm, base_of, diag, base = (
            sb(n, [P, NE]) for n in ("tot", "keyrow", "cmp", "perm", "base_of", "base_diag", "base"))
        rkc = sb("rank_consts", [P, 2 * NE + 1])
        keycol, rankcol, nbcol, basecol = (sb(n, [P, 1]) for n in ("keycol", "rankcol", "nbcol", "basecol"))
        nbi = sb("nbi", [P, 1], I32)
        starts = sb("starts", [P, PAIRS + 1])
        di, rowi, stepi = (sb(n, [P, NCH], I32) for n in ("di", "rowi", "stepi"))
        dest = sb("dest", [P, NCH, 2], U32)
        fill = sb("fill", [P, STEPS + 2], U32)
        rk = own.enter_context(nc.psum_tensor("rank_ps", [P, NCH * NE], F32))
        ip = own.enter_context(nc.psum_tensor("info_ps", [P, 512], F32))
        cb = own.enter_context(nc.psum_tensor("count_ps", [P, 512], F32))
        cn, ccol, nbr, basr = cb[:, 0:NE], cb[0:NE, NE:NE + 1], cb[:, 2 * NE:3 * NE], cb[:, 3 * NE:4 * NE]
        loaded, step, shifted, gexp, need_e2, e2, m_ready, rank_ps, perm_ready, order_ps, diag_ready, base_ps = map(
            sem, ("route_in", "route_step", "group_shifted", "group_exp", "gap_ready", "gap_exp", "choices_ready",
                  "rank_ps", "perm_ready", "order_ps", "diag_ready", "base_ps"))
        filled, dest_ready, scattered, table_in = map(sem, ("filled", "dest_ready", "scattered", "table_in"))
        fill_set, info_ready, ready = sem("fill_set"), sem("info_ready"), sem("route_ready")

        block = own.enter_context(nc.Block())

        @block.sync
        def _(sp):
            sp.dma_start(lg[:], dram["lg"].rearrange("t p e -> p t e")).then_inc(loaded, 16)
            sp.dma_start(ids0[:], dram["ids"]).then_inc(loaded, 16)
            sp.dma_start(io8[:], dram["io8"]).then_inc(loaded, 16)
            sp.dma_start(iop[:], dram["iop"]).then_inc(loaded, 16)
            sp.dma_start(rkc[:], dram["rkc"]).then_inc(loaded, 16)
            sp.wait_ge(fill_set, 1)
            sp.dma_start(dram["table"].rearrange("(p b) o -> p (b o)", p=P), fill[:]).then_inc(filled, 16)
            sp.wait_ge(info_ready, 2)
            for u in range(2):
                load_gate_up(sp, r, dram, experts_of(sp, r, 0, u), u, 16)
            sp.wait_ge(scattered, 16 * 2 * NCH)
            sp.dma_start(r.ids[:], dram["table"].rearrange("(p b) o -> p (b o)", p=P)).then_inc(table_in, 16)
            sp.wait_ge(table_in, 16)

        @block.gpsimd
        def _(pool):
            pool.memset(fill[:], FREE_ROW).then_inc(fill_set, 1)
            pool.wait_ge(filled, 16)
            pool.wait_ge(dest_ready, 2)
            for n in range(NCH):
                for k in range(2):
                    pool.indirect_dma_start(
                        out=dram["table"], out_offset=bass.IndirectOffsetOnAxis(ap=dest[:, n, k:k + 1], axis=0),
                        in_=ids0[:, n, k:k + 1].bitcast(U32), in_offset=None).then_inc(scattered, 16)
            pool.wait_ge(scattered, 16 * 2 * NCH)

        @block.scalar
        def _(act):
            act.wait_ge(shifted, 1)
            act.activation(ge[:], ge[:], ACT.Exp).then_inc(gexp, 1)
            act.wait_ge(need_e2, 1)
            act.activation(ew[:], ew[:], ACT.Exp).then_inc(e2, 1)

        @block.tensor
        def _(pe):
            pe.wait_ge(m_ready, 1)
            mmv = MM[:].rearrange("p t g e -> p (t g e)")
            ccv = CC[:].rearrange("p t g e -> p (t g e)")
            pe.matmul(cn, t.cst[:, C_ONE, :], tot[:], start=True, stop=True)
            pe.matmul(ccol, tot[:], t.cst[:, C_ONE, 0:1], start=True, stop=True).then_inc(rank_ps, 1)
            for half in range(2):
                c = slice(half * 512, half * 512 + 512)
                pe.matmul(rk[:, c], t.cst[:, C_US, :], mmv[:, c], start=True, stop=False)
                mm = pe.matmul(rk[:, c], t.cst[:, C_ONE, :], ccv[:, c], start=False, stop=True)
            mm.then_inc(rank_ps, 1)
            pe.wait_ge(perm_ready, 1)
            pe.matmul(nbr, nbcol[0:NE, :].to_broadcast([NE, P]), perm[0:NE, :], start=True, stop=True)
            pe.matmul(ip[0:1, 0:NE], iop[0:NE, :], perm[0:NE, :], start=True, stop=True).then_inc(order_ps, 1)
            pe.wait_ge(diag_ready, 1)
            pe.matmul(basr, t.cst[0:NE, C_ONE, :], diag[0:NE, :], start=True, stop=True).then_inc(base_ps, 1)

        @block.vector
        def _(dve):
            count = [0]

            def then(ins):
                count[0] += 1
                ins.then_inc(step, 1)
                dve.wait_ge(step, count[0])

            def onehot(values, top, out):
                then(dve.tensor_tensor(eq[:], values, over_cols(top, NG), ALU.is_equal))
                then(dve.scalar_tensor_tensor(eq[:], eq[:], -64.0, over_heads(io8[:, 1, :], NCH), ALU.mult, ALU.add))
                then(dve.tensor_reduce(ix[:], eq[:], AXX, ALU.min))
                then(dve.tensor_tensor(out, over_heads(io8[:, 0, :], NCH), over_cols(ix[:], NG), ALU.is_equal))

            dve.wait_ge(loaded, 80)
            G = lg[:, :, 0:NG]
            E = lg[:, :, NG:NR].rearrange("p t (g e) -> p t g e", g=NG)
            then(dve.tensor_reduce(gm[:], G, AXX, ALU.max))
            dve.tensor_tensor(ge[:], G, over_cols(gm[:], NG), ALU.subtract).then_inc(shifted, 1)
            onehot(G, gm[:], ohg[:])
            ohg4 = ohg[:].unsqueeze(3).to_broadcast([P, NCH, NG, EPG])
            then(dve.tensor_tensor(V[:], E, ohg4, ALU.mult))
            then(dve.tensor_reduce(sel[:], V[:].rearrange("p t g e -> p t e g"), AXX, ALU.add))
            then(dve.tensor_reduce(m1[:], sel[:], AXX, ALU.max))
            onehot(sel[:], m1[:], oh1[:])
            then(dve.scalar_tensor_tensor(sel2[:], oh1[:], -1e30, sel[:], ALU.mult, ALU.add))
            then(dve.tensor_reduce(m2[:], sel2[:], AXX, ALU.max))
            onehot(sel2[:], m2[:], oh2[:])
            dve.tensor_tensor(ew[:], m2[:], m1[:], ALU.subtract).then_inc(need_e2, 1)
            then(dve.tensor_tensor(M1[:], ohg4, oh1[:].unsqueeze(2).to_broadcast([P, NCH, NG, EPG]), ALU.mult))
            then(dve.tensor_tensor(M2[:], ohg4, oh2[:].unsqueeze(2).to_broadcast([P, NCH, NG, EPG]), ALU.mult))
            then(dve.tensor_tensor(MM[:], M1[:], M2[:], ALU.add))
            then(dve.memset(CC[:, 0], 0.0))
            for n in range(1, NCH):
                then(dve.tensor_tensor(CC[:, n], CC[:, n - 1], MM[:, n - 1], ALU.add))
            dve.tensor_tensor(tot[:].rearrange("p (g e) -> p g e", g=NG), CC[:, NCH - 1], MM[:, NCH - 1],
                              ALU.add).then_inc(m_ready, 1)
            dve.wait_ge(rank_ps, 1)
            then(dve.scalar_tensor_tensor(keyrow[:], cn, float(NE), rkc[:, 0:NE], ALU.mult, ALU.add))
            then(dve.scalar_tensor_tensor(keycol[0:NE, :], ccol, float(NE), rkc[0:NE, 2 * NE:], ALU.mult, ALU.add))
            then(dve.tensor_scalar(nbi[0:NE, :], ccol, float(HB - 1), None, ALU.add))
            then(dve.tensor_scalar(nbi[0:NE, :], nbi[0:NE, :], 6, None, ALU.logical_shift_right))
            then(dve.tensor_copy(nbcol[0:NE, :], nbi[0:NE, :]))
            then(dve.tensor_scalar(cmp_[0:NE, :], keyrow[0:NE, :], keycol[0:NE, :], None, ALU.is_gt))
            then(dve.tensor_reduce(rankcol[0:NE, :], cmp_[0:NE, :], AXX, ALU.add))
            then(dve.memset(starts[:, 0:1], 0.0))
            dve.tensor_scalar(perm[0:NE, :], rkc[0:NE, NE:2 * NE], rankcol[0:NE, :], None,
                              ALU.is_equal).then_inc(perm_ready, 1)
            dve.wait_ge(order_ps, 1)
            dve.wait_ge(perm_ready, 1)
            then(dve.tensor_tensor_scan(starts[:, 1:], t.cst[:, C_ONE, 0:PAIRS], nbr.rearrange("p (r s) -> p s r", s=2)[:, 0, :],
                                        0.0, ALU.mult, ALU.add))
            dve.tensor_copy(r.info[0:1, 0:NE], ip[0:1, 0:NE]).then_inc(info_ready, 1)
            dve.tensor_copy(r.info[0:1, NE:], starts[0:1, :]).then_inc(info_ready, 1)
            bo = base_of[0:NE, :].rearrange("p (r s) -> p r s", s=2)
            for side in range(2):
                then(dve.tensor_scalar(bo[:, :, side], starts[0:NE, 0:PAIRS], float(HB), float(side * SIDE), ALU.mult,
                                       ALU.add))
            then(dve.tensor_tensor(base_of[0:NE, :], base_of[0:NE, :], perm[0:NE, :], ALU.mult))
            then(dve.tensor_reduce(basecol[0:NE, :], base_of[0:NE, :], AXX, ALU.add))
            dve.tensor_scalar(diag[0:NE, :], t.cst[0:NE, C_ID, 0:NE], basecol[0:NE, :], None,
                              ALU.mult).then_inc(diag_ready, 1)
            dve.wait_ge(base_ps, 1)
            then(dve.tensor_copy(base[:], basr))
            dve.wait_ge(rank_ps, 2)
            v3 = V[:].rearrange("p t g e -> p t (g e)")
            then(dve.tensor_tensor(v3, rk[:].rearrange("p (t e) -> p t e", t=NCH), over_heads(base[:], NCH), ALU.add))
            for k, M in enumerate((M1, M2)):
                then(dve.tensor_tensor(M[:], M[:], V[:], ALU.mult))
                then(dve.tensor_reduce(dk[:], M[:].rearrange("p t g e -> p t (g e)"), AXX, ALU.add))
                then(dve.tensor_copy(di[:], dk[:]))
                then(dve.tensor_scalar(rowi[:], di[:], HB - 1, None, ALU.bitwise_and))
                then(dve.tensor_scalar(stepi[:], di[:], SIDE - 1, None, ALU.bitwise_and))
                then(dve.tensor_scalar(stepi[:], stepi[:], 6, None, ALU.logical_shift_right))
                then(dve.tensor_scalar(di[:], di[:], 13, None, ALU.logical_shift_right))
                then(dve.scalar_tensor_tensor(rowi[:], di[:], float(HB), rowi[:], ALU.mult, ALU.add))
                dve.scalar_tensor_tensor(dest[:, :, k], rowi[:], float(STEPS + 2), stepi[:], ALU.mult,
                                         ALU.add).then_inc(dest_ready, 1)
                dve.wait_ge(dest_ready, k + 1)
            dve.wait_ge(gexp, 1)
            then(dve.tensor_reduce(gs[:], ge[:], AXX, ALU.add))
            dve.wait_ge(e2, 1)
            then(dve.scalar_tensor_tensor(gs[:], ew[:], 1.0, gs[:], ALU.add, ALU.mult))
            then(dve.reciprocal(r.wts[:, :, 0], gs[:]))
            then(dve.tensor_tensor(r.wts[:, :, 1], r.wts[:, :, 0], ew[:], ALU.mult))
            dve.wait_ge(info_ready, 2)
            dve.wait_ge(table_in, 16)
            dve.tensor_scalar(r.tok[:].bitcast(I32), r.ids[:].bitcast(I32), 1, None,
                              ALU.logical_shift_right).then_inc(ready, 1)
            dve.wait_ge(ready, 1)


def build_experts(nc, r, t, dram):
    with ExitStack() as own:
        def sb(name, shape, dt=F32):
            return own.enter_context(nc.sbuf_tensor(name, shape, dt))

        def sem(name):
            return t.ctx.enter_context(nc.semaphore(name))

        wdn = sb("wdn", [P, SLOTS, KE, D])
        xg, xT = sb("xg", [P, D]), sb("xT", [P, KD, P])
        hs, hT = sb("hid", [P, DE]), sb("hidT", [P, KE, P])
        y = sb("y", [P, D])
        gcol, scol = sb("gather_rows", [P, 1], U32), sb("scatter_rows", [P, 1], U32)
        gate, up = (own.enter_context(nc.psum_tensor(n, [P, DE], F32)) for n in ("gate_ps", "up_ps"))
        xp = [own.enter_context(nc.psum_tensor(f"xT{n}_ps", [P, 4, P], F32)) for n in range(2)]
        hp = own.enter_context(nc.psum_tensor("hidT_ps", [P, KE, P], F32))
        yp = [own.enter_context(nc.psum_tensor(f"y{n}_ps", [P, 512], F32)) for n in range(2)]

        (cleared, gcol_set, scol_set, x_in, y_out, xT_ps, xT_ready, gate_done, up_done, silu_done, hid_ready,
         hidT_done, hidT_ready, y0_done, y1_done, y0_ready, y1_ready) = map(sem, (
            "xg_cleared", "gather_rows_set", "scatter_rows_set", "x_in", "y_out", "xT_done", "xT_ready", "gate_done",
            "up_done", "silu_done", "hid_ready", "hidT_done", "hidT_ready", "y0_done", "y1_done", "y0_ready",
            "y1_ready"))
        y_done, y_ready = (y0_done, y1_done), (y0_ready, y1_ready)
        ident = t.cst[:, C_ID, :]
        sides = (slice(0, HB), slice(HB, P))

        def start_of(eng, pair):
            return eng.value_load(r.info[0:1, bass.ds(pair + NE, 1)], min_val=0, max_val=STEPS)

        def steps_of(eng):
            return eng.value_load(r.info[0:1, NE + PAIRS:NE + PAIRS + 1], min_val=2 * SEQ // P, max_val=STEPS)

        block = own.enter_context(nc.Block())

        @block.sync
        def _(sp):
            def load(i, u):
                experts = experts_of(sp, r, i, u)
                first = isinstance(i, int)
                landed = 16
                if not first:
                    end = start_of(sp, 2 * i + u - 1)
                    sp.reg_mul(counts[0], i, 16)
                    sp.reg_add(counts[1], counts[0], 16)
                    before, landed = (sp.snap(x) for x in counts)
                    for side in range(2):
                        sp.wait_ge(r.dn_in[1 - u][side], landed if u else before)
                        sp.wait_ge(r.gate_in[u][side], before)
                        sp.wait_ge(r.up_in[u][side], before)
                    sp.wait_ge(up_done, end)
                    load_gate_up(sp, r, dram, experts, u, landed)
                    sp.wait_ge(y1_done, end)
                for side in range(2):
                    sp.wait_ge(r.up_in[u][side], landed)
                    sp.dma_start(wdn[:, 2 * u + side].rearrange("p k d -> p (k d)"),
                                 dram["w_down"][bass.ds(experts[side], 1)].rearrange(
                                     "o (p k) d -> p (o k d)", p=P)).then_inc(r.dn_in[u][side], 16)

            counts = [sp.alloc_register(n) for n in ("landed_before", "landed")]
            load(0, 0)
            load(0, 1)
            with sp.Fori(1, PAIRS // 2) as i:
                load(i, 0)
                load(i, 1)
            for u in range(2):
                for side in range(2):
                    for weights_in in (r.gate_in, r.up_in, r.dn_in):
                        sp.wait_ge(weights_in[u][side], 16 * (PAIRS // 2))

        @block.gpsimd
        def _(pool):
            steps = steps_of(pool)

            def gather(s):
                pool.wait_ge(x_in, 16 * s)
                pool.wait_ge(xT_ps, 2 * s)
                pool.tensor_copy(gcol[:], r.tok[:, bass.ds(s, 1)]).then_inc(gcol_set, 1)
                pool.wait_ge(gcol_set, s + 1)
                pool.wait_ge(cleared, 1)
                pool.indirect_dma_start(out=xg[:], out_offset=None, in_=dram["h2"],
                                        in_offset=bass.IndirectOffsetOnAxis(ap=gcol[:], axis=0),
                                        bounds_check=s + (SEQ - 1), oob_is_err=False).then_inc(x_in, 16)

            def scatter(s):
                pool.wait_ge(y_out, 16 * s)
                pool.tensor_copy(scol[:], r.ids[:, bass.ds(s, 1)]).then_inc(scol_set, 1)
                pool.wait_ge(scol_set, s + 1)
                pool.wait_ge(y0_ready, s + 1)
                pool.wait_ge(y1_ready, s + 1)
                pool.wait_ge(cleared, 1)
                pool.indirect_dma_start(out=dram["y"], out_offset=bass.IndirectOffsetOnAxis(ap=scol[:], axis=0),
                                        in_=y[:], in_offset=None,
                                        bounds_check=s + (2 * SEQ - 1), oob_is_err=False).then_inc(y_out, 16)

            pool.memset(xg[:], 0.0).then_inc(cleared, 1)
            pool.wait_ge(cleared, 1)
            gather(0)
            with pool.Fori(0, steps) as s:
                gather(s + 1)
                scatter(s)
            pool.wait_ge(x_in, 16 * (steps + 1))
            pool.wait_ge(y_out, 16 * steps)

        @block.tensor
        def _(pe):
            def x_transposes(s, half):
                if half == 0:
                    pe.wait_ge(x_in, 16 * (s + 1))
                    pe.wait_ge(xT_ready, s)
                xv = xg[:].rearrange("p (q k) -> p k q", k=KD)
                for k in range(4 * half, 4 * half + 4):
                    mm = pe.transpose(xp[half][:, k % 4, :], xv[:, k, :], ident)
                mm.then_inc(xT_ps, 1)

            def gate_up(s, u, m):
                out, before, done = ((gate, silu_done, gate_done), (up, hid_ready, up_done))[m]
                if m == 0:
                    pe.wait_ge(xT_ready, s + 1)
                pe.wait_ge(before, s)
                for k in range(KD):
                    for side in range(2):
                        mm = pe.matmul(out[sides[side], :], xT[:, k, sides[side]], r.wgu[:, 2 * u + side, m * KD + k, :],
                                       start=(k == 0), stop=(k == KD - 1))
                mm.then_inc(done, 1)

            def hid_transposes(s):
                pe.wait_ge(hid_ready, s + 1)
                pe.wait_ge(hidT_ready, s)
                hv = hs[:].rearrange("p (q k) -> p k q", k=KE)
                for k in range(KE):
                    mm = pe.transpose(hp[:, k, :], hv[:, k, :], ident)
                mm.then_inc(hidT_done, 1)

            def down(s, u, half):
                pe.wait_ge(hidT_ready, s + 1)
                pe.wait_ge(y_ready[half], s)
                for k in range(KE):
                    for side in range(2):
                        mm = pe.matmul(yp[half][sides[side], :], hT[:, k, sides[side]],
                                       wdn[:, 2 * u + side, k, half * 512:(half + 1) * 512],
                                       start=(k == 0), stop=(k == KE - 1))
                mm.then_inc(y_done[half], 1)

            x_transposes(0, 0)
            x_transposes(0, 1)
            with pe.Fori(0, PAIRS // 2) as i:
                for u in range(2):
                    first, end = start_of(pe, 2 * i + u), start_of(pe, 2 * i + u + 1)
                    with pe.Fori(first, end) as s:
                        pe.wait_ge(r.gate_in[u][0], 16 * (i + 1))
                        pe.wait_ge(r.gate_in[u][1], 16 * (i + 1))
                        gate_up(s, u, 0)
                        pe.wait_ge(r.up_in[u][0], 16 * (i + 1))
                        pe.wait_ge(r.up_in[u][1], 16 * (i + 1))
                        gate_up(s, u, 1)
                        x_transposes(s + 1, 0)
                        hid_transposes(s)
                        x_transposes(s + 1, 1)
                        pe.wait_ge(r.dn_in[u][0], 16 * (i + 1))
                        pe.wait_ge(r.dn_in[u][1], 16 * (i + 1))
                        down(s, u, 0)
                        down(s, u, 1)

        @block.scalar
        def _(act):
            steps = steps_of(act)

            def x_evac(s):
                act.wait_ge(xT_ps, 2 * (s + 1))
                act.wait_ge(up_done, s)
                for k in range(KD):
                    ins = act.activation(xT[:, k, :], xp[k // 4][:, k % 4, :], ACT.Identity,
                                         bias=t.B2[:, k:k + 1], scale=t.A2[:, k:k + 1])
                ins.then_inc(xT_ready, 1)

            def silu(s):
                act.wait_ge(gate_done, s + 1)
                act.wait_ge(hidT_done, s)
                act.activation(hs[:], gate[:], ACT.Silu).then_inc(silu_done, 1)

            def hid_evac(s):
                act.wait_ge(hidT_done, s + 1)
                act.wait_ge(y1_done, s)
                act.copy(hT[:], hp[:]).then_inc(hidT_ready, 1)

            x_evac(0)
            with act.Fori(0, steps) as s:
                silu(s)
                hid_evac(s)
                x_evac(s + 1)

        @block.vector
        def _(dve):
            steps = steps_of(dve)
            with dve.Fori(0, steps) as s:
                dve.wait_ge(up_done, s + 1)
                dve.wait_ge(silu_done, s + 1)
                dve.tensor_tensor(hs[:], hs[:], up[:], ALU.mult).then_inc(hid_ready, 1)
                for half in range(2):
                    dve.wait_ge(y_done[half], s + 1)
                    dve.wait_ge(y_out, 16 * s)
                    dve.tensor_copy(y[:, half * 512:(half + 1) * 512], yp[half][:]).then_inc(y_ready[half], 1)


def build_combine(nc, r, t, dram):
    with ExitStack() as own:
        TILES = 4

        def sb(name, shape, dt=F32):
            return own.enter_context(nc.sbuf_tensor(name, shape, dt))

        def sem(name):
            return t.ctx.enter_context(nc.semaphore(name))

        def four(make, name, *a):
            return [make(f"{name}{u}", *a) for u in range(TILES)]

        G2 = sb("G2", [P, D])
        yy, xx, oo = four(sb, "yy", [P, 2, D]), four(sb, "xx", [P, D]), four(sb, "oo", [P, D])
        junk = four(sb, "junk2_", [P, D], BF16)
        ss, var, rs = four(sb, "css", [P, 1]), four(sb, "cvar", [P, 1]), four(sb, "crs", [P, 1])
        hp = sb("half_pow2", [P, 2])
        g2_in, hp_set = sem("g2_in"), sem("half_pow_set")
        y_in, x_in, first, moe, ss_done, var_done, rs_done, scaled, added, stored = (four(sem, n) for n in (
            "cy_in", "cx_in", "first_weighted", "moe_ready", "c_ss", "c_var", "c_rstd", "c_scaled", "c_added", "c_stored"))
        yd = dram["y"].rearrange("(n p k) d -> n p k d", p=P, k=2)
        x1d = dram["x1"].rearrange("(n p) d -> n p d", p=P)
        od = dram["out"].rearrange("o (n p) d -> (o n) p d", p=P)
        TURNS = NCH // TILES

        block = own.enter_context(nc.Block())

        @block.sync
        def _(sp):
            sp.dma_start(G2[:], dram["g2"].to_broadcast([P, D])).then_inc(g2_in, 16)
            with sp.Fori(0, TURNS) as i:
                for u in range(TILES):
                    sp.wait_ge(moe[u], i)
                    sp.dma_start(yy[u][:], yd[bass.ds(TILES * i + u, 1)].rearrange("o p k d -> (o p) k d")).then_inc(y_in[u], 16)
                    sp.wait_ge(added[u], i)
                    sp.dma_start(xx[u][:], x1d[bass.ds(TILES * i + u, 1)].rearrange("o p d -> (o p) d")).then_inc(x_in[u], 16)

        @block.scalar
        def _(act):
            with act.Fori(0, TURNS) as i:
                for u in range(TILES):
                    act.wait_ge(moe[u], i + 1)
                    act.activation(junk[u][:], oo[u][:], ACT.Square, accum_out=ss[u][:]).then_inc(ss_done[u], 1)
                for u in range(TILES):
                    act.wait_ge(added[u], i + 1)
                    act.dma_start(od[bass.ds(TILES * i + u, 1)].rearrange("o p d -> (o p) d"), oo[u][:]).then_inc(stored[u], 16)
            for u in range(TILES):
                act.wait_ge(stored[u], 16 * TURNS)

        @block.gpsimd
        def _(pool):
            pool.memset(hp[:, 0:1], -0.5)
            pool.memset(hp[:, 1:2], D * EPS).then_inc(hp_set, 1)
            pool.wait_ge(hp_set, 1)
            with pool.Fori(0, TURNS) as i:
                for u in range(TILES):
                    pool.wait_ge(ss_done[u], i + 1)
                    pool.tensor_tensor(var[u][:], ss[u][:], hp[:, 1:2], ALU.add).then_inc(var_done[u], 1)
                    pool.wait_ge(var_done[u], i + 1)
                    pool.tensor_tensor(rs[u][:], var[u][:], hp[:, 0:1], ALU.pow).then_inc(rs_done[u], 1)

        @block.vector
        def _(dve):
            dve.wait_ge(g2_in, 16)
            with dve.Fori(0, TURNS) as i:
                for u in range(TILES):
                    w = r.wts[:, bass.ds(TILES * i + u, 1), :].rearrange("p o k -> p (o k)")
                    dve.wait_ge(y_in[u], 16 * (i + 1))
                    dve.wait_ge(stored[u], 16 * i)
                    dve.tensor_scalar(oo[u][:], yy[u][:, 0, :], w[:, 0:1], None, ALU.mult).then_inc(first[u], 1)
                    dve.wait_ge(first[u], i + 1)
                    dve.scalar_tensor_tensor(oo[u][:], yy[u][:, 1, :], w[:, 1:2], oo[u][:], ALU.mult,
                                             ALU.add).then_inc(moe[u], 1)
                for u in range(TILES):
                    dve.wait_ge(rs_done[u], i + 1)
                    dve.scalar_tensor_tensor(oo[u][:], oo[u][:], rs[u][:], G2[:], ALU.mult, ALU.mult).then_inc(scaled[u], 1)
                    dve.wait_ge(scaled[u], i + 1)
                    dve.wait_ge(x_in[u], 16 * (i + 1))
                    dve.tensor_tensor(oo[u][:], oo[u][:], xx[u][:], ALU.add).then_inc(added[u], 1)


class Tiles:
    pass


def build(nc, dram):
    with ExitStack() as ctx:
        def sb(where, name, shape, dt=F32):
            return where.enter_context(nc.sbuf_tensor(name, shape, dt))

        t, r = Tiles(), Tiles()
        t.ctx = ctx
        t.cst = sb(ctx, "cst", [P, C_MATS, P])
        t.A2, t.B2 = sb(ctx, "A2", [P, KD]), sb(ctx, "B2", [P, KD])
        with ExitStack() as mix:
            t.A1, t.B1 = sb(mix, "A1", [P, KD]), sb(mix, "B1", [P, KD])
            t.chp = sb(mix, "chp", [P, CH_COLS])
            t.G1 = sb(mix, "G1", [P, D])
            t.dnn = sb(mix, "dnn", [P, HD])
            t.gaterow, t.babias = sb(mix, "gaterow", [P, 2 * HEADS]), sb(mix, "babias", [P, 2 * HEADS])
            t.nega, t.halfb = sb(mix, "nega", [P, HEADS]), sb(mix, "halfb", [P, 2 * CFG])
            t.rbias = sb(mix, "rbias", [P, NR])
            t.wr = sb(mix, "wr", [P, KD, NR])
            t.win, t.wout = sb(mix, "win", [P, KD, IN_COLS]), sb(mix, "wout", [P, KD, D])
            build_setup(nc, mix, t, dram)
            build_mixer(nc, t, dram)
        r.ids, r.tok = sb(ctx, "ids", [P, STEPS + 2], U32), sb(ctx, "tok", [P, STEPS + 2], U32)
        r.info = sb(ctx, "info", [1, NE + PAIRS + 1], I32)
        r.wts = sb(ctx, "wts", [P, NCH, 2])
        r.wgu = sb(ctx, "wgu", [P, SLOTS, 2 * KD, DE])
        r.gate_in, r.up_in, r.dn_in = (
            [[ctx.enter_context(nc.semaphore(f"{n}{u}{side}")) for side in range(2)] for u in range(2)]
            for n in ("gate_in", "up_in", "down_in"))
        build_routing(nc, r, t, dram)
        build_experts(nc, r, t, dram)
        build_combine(nc, r, t, dram)


def _constants():
    p, c = np.arange(P)[:, None], np.arange(P)[None, :]
    mats = [p == c, c >= p, c > p, c < p, np.ones((P, P))]
    mats += [(((p ^ c) >> n) == 1) & (c > p) for n in range(LEVELS)]
    cst = np.stack(mats, axis=1).astype(np.float32)
    pair = np.stack([np.arange(PAIRS // 2), PAIRS - 1 - np.arange(PAIRS // 2)], axis=1).reshape(-1)
    rank_at = (2 * pair[:, None] + np.arange(2)[None, :]).reshape(-1)
    rkc = np.concatenate([np.broadcast_to(NE - 1 - np.arange(NE), (P, NE)), np.broadcast_to(rank_at, (P, NE)),
                          NE - 1 - np.arange(P)[:, None]], axis=1).astype(np.float32)
    io8 = np.broadcast_to(np.stack([np.arange(8), np.arange(8) + 64]), (P, 2, 8)).astype(np.float32)
    iop = np.arange(P, dtype=np.float32)[:, None]
    tok = np.arange(NCH)[None, :] * P + np.arange(P)[:, None]
    ids = np.stack([2 * tok, 2 * tok + 1], axis=2).astype(np.int32)
    return {"cst": cst, "io8": io8, "iop": iop, "ids": ids, "rkc": rkc}


def kernel(**inputs):
    import concourse.bacc as _bacc
    from concourse.bass_utils import run_bass_kernel_spmd as _run

    a = {n: np.asarray(v) for n, v in inputs.items()}

    def cols(v):
        return np.swapaxes(v.reshape((-1, P) + v.shape[1:]), 0, 1)

    def flat(v):
        return np.ascontiguousarray(v).reshape(P, -1)

    chp = np.concatenate([
        flat(cols(a["c"][0])), flat(cols(a["norm_pre_mix"][0])), flat(a["norm_pre_ffn"][0].reshape(P, KD)),
        flat(cols(a["dn_conv_w"][0].T)), flat(cols(a["cf_pw1_b"][0])), flat(cols(a["cf_dw_w"][0].T)),
        flat(cols(a["cf_dw_b"][0])), flat(cols(a["cf_ln_w"][0])), flat(cols(a["cf_ln_b"][0]))], axis=1)
    rows = np.concatenate([a[n][0].reshape(-1) for n in (
        "b_ada", "norm_post_mix", "norm_post_ffn", "dn_norm_w", "dn_a_log", "dn_dt_bias",
        "b_router_group", "b_router_expert")])[None, :]
    w_r = np.concatenate([a["w_router_group"][0], a["w_router_expert"][0]], axis=1).reshape(P, KD, NR)
    feeds = {"x": a["x"][0], "chp": chp, "rows": rows, "w_ada": a["w_ada"][0], "w_in": cols(a["w_in"][0]),
             "w_out": cols(a["w_out"][0]), "w_r": w_r, "w_gate": a["w_gate"][0], "w_up": a["w_up"][0],
             "w_down": a["w_down"][0]}
    feeds.update(_constants())

    nc = _bacc.Bacc("TRN2", target_bir_lowering=False, num_devices=1, dynamic_dma_scratch_size=2048)
    arrays, dram = {}, {}
    for n, v in feeds.items():
        v = np.ascontiguousarray(v)
        arrays[f"in_{n}_dram"] = v
        dram[n] = nc.dram_tensor(f"in_{n}_dram", v.shape, mybir.dt.from_np(v.dtype), kind="ExternalInput").ap()
    for n, shape, dt in (("x1", (SEQ, D), F32), ("h2", (SEQ, D), F32), ("y", (2 * SEQ, D), F32),
                         ("lg", (NCH, P, NR), F32), ("g2", (1, D), F32), ("table", (P * (STEPS + 2), 1), U32)):
        dram[n] = nc.dram_tensor(f"{n}_dram", shape, dt, kind=SCRATCH).ap()
    dram["out"] = nc.dram_tensor("out_0_dram", (1, SEQ, D), F32, kind="ExternalOutput").ap()
    build(nc, dram)
    got = _run(nc, [arrays], core_ids=[0])
    return got.results[0]["out_0_dram"]
```
